# Optimizing a Trainium2 kernel written in Bass

```python
import math
import jax
import jax.numpy as jnp
from jax import lax
import numpy as np

D_MODEL = 1024
BATCH = 1
SEQ = 256
DEPTH = 1

EPS = 1e-6
NEG_INF = -1e30
FORCE_BONUS = 1e4

NSA_HEADS = 8
NSA_KV_GROUPS = 2
NSA_HPG = NSA_HEADS // NSA_KV_GROUPS
NSA_HEAD_DIM = 64
CMP_BLOCK = 32
CMP_STRIDE = 16
CMP_HIDDEN = 128
SEL_BLOCK = 64
SEL_TOPK = 16
N_LOCAL_FORCED = 2
WINDOW = 512
SEL_Q_CHUNK = 64
Q_BLOCK = 128

MLA_HEADS = 8
MLA_Q_LORA = 256
MLA_KV_LORA = 128
MLA_NOPE_DIM = 64
MLA_ROPE_DIM = 32
MLA_V_DIM = 64
ROPE_THETA = 10000.0

PEER_HEADS = 8
PEER_N_KEYS = 128
PEER_N_EXPERTS = PEER_N_KEYS * PEER_N_KEYS
PEER_QUERY_DIM = 256
PEER_TOPK = 16
PEER_TOKEN_CHUNK = 256

NSA_Q_W = NSA_HEADS * NSA_HEAD_DIM
NSA_KV_W = NSA_KV_GROUPS * NSA_HEAD_DIM
NSA_GATE_W = 3 * NSA_HEADS
MLA_OUT_W = MLA_HEADS * MLA_V_DIM
IN_SPLITS = (NSA_Q_W, NSA_KV_W, NSA_KV_W, NSA_KV_W, NSA_KV_W, NSA_KV_W, NSA_KV_W, NSA_GATE_W,
             MLA_Q_LORA, MLA_KV_LORA, MLA_ROPE_DIM, D_MODEL, D_MODEL)
IN_WIDTH = sum(IN_SPLITS)

kernel_name = 'nsa_mla_peer_hybrid_block'

def rms_norm(x, g):
    xf = x.astype(jnp.float32)
    y = xf * lax.rsqrt(jnp.mean(xf * xf, axis=-1, keepdims=True) + EPS)
    return (y * g.astype(jnp.float32)).astype(x.dtype)

def masked_softmax(s, mask):
    s = jnp.where(mask, s.astype(jnp.float32), NEG_INF)
    m = jnp.max(s, axis=-1, keepdims=True)
    p = jnp.where(mask, jnp.exp(s - m), 0.0)
    return p / jnp.maximum(jnp.sum(p, axis=-1, keepdims=True), 1e-30)

def alibi_slopes(n):
    return 2.0 ** (-8.0 * jnp.arange(1, n + 1, dtype=jnp.float32) / n)

def rope_cos_sin(positions, dim):
    inv = ROPE_THETA ** (-jnp.arange(0, dim, 2, dtype=jnp.float32) / dim)
    ang = positions.astype(jnp.float32)[..., None] * inv
    return jnp.cos(ang), jnp.sin(ang)

def apply_rope(x, cos, sin):
    x1, x2 = jnp.split(x.astype(jnp.float32), 2, axis=-1)
    return jnp.concatenate([x1 * cos - x2 * sin, x1 * sin + x2 * cos], axis=-1)

def _to_chunks(a, axis, n):
    shp = a.shape
    a = a.reshape(shp[:axis] + (n, shp[axis] // n) + shp[axis + 1:])
    return jnp.moveaxis(a, axis, 0)

def _from_chunks(a, axis):
    a = jnp.moveaxis(a, 0, axis)
    shp = a.shape
    return a.reshape(shp[:axis] + (shp[axis] * shp[axis + 1],) + shp[axis + 2:])

def _split_columns(a, sizes):
    offsets = np.cumsum(np.array(sizes))[:-1].tolist()
    return jnp.split(a, offsets, axis=-1)

def nsa_compress(kv_heads, pos_emb, w1, w2):
    T = kv_heads.shape[2]
    nc = (T - CMP_BLOCK) // CMP_STRIDE + 1
    idx = jnp.arange(nc)[:, None] * CMP_STRIDE + jnp.arange(CMP_BLOCK)[None, :]
    blocks = kv_heads[:, :, idx, :] + pos_emb.astype(jnp.float32)
    flat = blocks.reshape(blocks.shape[:3] + (CMP_BLOCK * NSA_HEAD_DIM,))
    return jax.nn.gelu(flat @ w1.astype(jnp.float32)) @ w2.astype(jnp.float32)

def nsa_attention(q, k_cmp, v_cmp, k_sel, v_sel, k_win, v_win, gate_logits,
                  cmp_pos_k, cmp_w1_k, cmp_w2_k, cmp_pos_v, cmp_w1_v, cmp_w2_v):
    f32 = jnp.float32
    B, T, _ = q.shape
    G, HPG, dk = NSA_KV_GROUPS, NSA_HPG, NSA_HEAD_DIM
    slopes = alibi_slopes(NSA_HEADS).reshape(G, HPG)
    pos = jnp.arange(T)
    qh = q.astype(f32).reshape(B, T, G, HPG, dk).transpose(0, 2, 3, 1, 4) * (dk ** -0.5)

    def heads(a):
        return a.astype(f32).reshape(B, T, G, dk).transpose(0, 2, 1, 3)

    kc = nsa_compress(heads(k_cmp), cmp_pos_k, cmp_w1_k, cmp_w2_k)
    vc = nsa_compress(heads(v_cmp), cmp_pos_v, cmp_w1_v, cmp_w2_v)
    nc = kc.shape[2]
    cmp_start = jnp.arange(nc) * CMP_STRIDE
    dist_c = pos[:, None] - (cmp_start + CMP_BLOCK - 1)[None, :]
    s_c = jnp.einsum('bghtd,bgnd->bghtn', qh, kc) - slopes[None, :, :, None, None] * dist_c
    p_c = masked_softmax(s_c, dist_c >= 0)
    o_cmp = jnp.einsum('bghtn,bgnd->bghtd', p_c, vc)

    ns = T // SEL_BLOCK
    sel_start = jnp.arange(ns) * SEL_BLOCK
    overlap = jnp.clip(jnp.minimum(cmp_start[:, None] + CMP_BLOCK, sel_start[None, :] + SEL_BLOCK)
                       - jnp.maximum(cmp_start[:, None], sel_start[None, :]), 0, None).astype(f32) / CMP_BLOCK
    importance = jnp.einsum('bghtn,ns->bgts', p_c, overlap)
    back = (pos // SEL_BLOCK)[:, None] - jnp.arange(ns)[None, :]
    causal_blk = back >= 0
    forced = causal_blk & ((back < N_LOCAL_FORCED) | (jnp.arange(ns)[None, :] == 0))
    sel_score = jnp.where(causal_blk, importance + FORCE_BONUS * forced.astype(f32), NEG_INF)
    top_s, sel_idx = lax.top_k(sel_score, min(SEL_TOPK, ns))
    sel_ok = top_s > 0.5 * NEG_INF
    ks_blocks = heads(k_sel).reshape(B, G, ns, SEL_BLOCK, dk)
    vs_blocks = heads(v_sel).reshape(B, G, ns, SEL_BLOCK, dk)
    bi = jnp.arange(B)[:, None, None, None]
    gi = jnp.arange(G)[None, :, None, None]

    def sel_chunk(args):
        qc, idx, ok, tq = args
        c, k = idx.shape[2], idx.shape[3]
        kg = ks_blocks[bi, gi, idx]
        vg = vs_blocks[bi, gi, idx]
        s = jnp.einsum('bghqd,bgqkld->bghqkl', qc, kg)
        kpos = idx[..., None] * SEL_BLOCK + jnp.arange(SEL_BLOCK)
        dist = tq[None, None, :, None, None] - kpos
        mask = ok[..., None] & (dist >= 0)
        s = s - slopes[None, :, :, None, None, None] * dist[:, :, None]
        p = masked_softmax(s.reshape(B, G, HPG, c, k * SEL_BLOCK), mask.reshape(B, G, 1, c, k * SEL_BLOCK))
        return jnp.einsum('bghqm,bgqmd->bghqd', p, vg.reshape(B, G, c, k * SEL_BLOCK, dk))

    nq = T // SEL_Q_CHUNK
    o_sel = _from_chunks(lax.map(sel_chunk, (_to_chunks(qh, 3, nq), _to_chunks(sel_idx, 2, nq),
                                             _to_chunks(sel_ok, 2, nq), pos.reshape(nq, SEL_Q_CHUNK))), 3)

    nb = T // Q_BLOCK
    kw_all = heads(k_win)
    vw_all = heads(v_win)
    band = jnp.arange(nb)[:, None] * Q_BLOCK - WINDOW + jnp.arange(WINDOW + Q_BLOCK)[None, :]

    def win_chunk(args):
        qc, kpos, tq = args
        kidx = jnp.clip(kpos, 0, T - 1)
        kb = kw_all[:, :, kidx]
        vb = vw_all[:, :, kidx]
        s = jnp.einsum('bghqd,bgkd->bghqk', qc, kb)
        dist = tq[:, None] - kpos[None, :]
        mask = (kpos[None, :] >= 0) & (dist >= 0) & (dist < WINDOW)
        s = s - slopes[None, :, :, None, None] * dist
        return jnp.einsum('bghqk,bgkd->bghqd', masked_softmax(s, mask), vb)

    o_win = _from_chunks(lax.map(win_chunk, (_to_chunks(qh, 3, nb), band, pos.reshape(nb, Q_BLOCK))), 3)

    gates = jax.nn.sigmoid(gate_logits.astype(f32)).reshape(B, T, 3, G, HPG).transpose(2, 0, 3, 4, 1)[..., None]
    o = gates[0] * o_cmp + gates[1] * o_sel + gates[2] * o_win
    return o.transpose(0, 3, 1, 2, 4).reshape(B, T, NSA_Q_W).astype(q.dtype)

def mla_attention(c_q, c_kv, k_rope, positions, q_norm_g, kv_norm_g, w_uq, w_ukv):
    f32 = jnp.float32
    B, T, _ = c_q.shape
    H = MLA_HEADS
    q = (rms_norm(c_q, q_norm_g) @ w_uq).astype(f32).reshape(B, T, H, MLA_NOPE_DIM + MLA_ROPE_DIM)
    kv = (rms_norm(c_kv, kv_norm_g) @ w_ukv).astype(f32).reshape(B, T, H, MLA_NOPE_DIM + MLA_V_DIM)
    q_nope, q_pe = q[..., :MLA_NOPE_DIM], q[..., MLA_NOPE_DIM:]
    k_nope, v = kv[..., :MLA_NOPE_DIM], kv[..., MLA_NOPE_DIM:]
    cos, sin = rope_cos_sin(positions, MLA_ROPE_DIM)
    q_pe = apply_rope(q_pe, cos[:, :, None], sin[:, :, None])
    k_pe = apply_rope(k_rope, cos, sin)
    qf = jnp.concatenate([q_nope, q_pe], axis=-1) * ((MLA_NOPE_DIM + MLA_ROPE_DIM) ** -0.5)
    kf = jnp.concatenate([k_nope, jnp.broadcast_to(k_pe[:, :, None, :], (B, T, H, MLA_ROPE_DIM))], axis=-1)
    qh = qf.transpose(0, 2, 1, 3)
    kh = kf.transpose(0, 2, 1, 3)
    vh = v.transpose(0, 2, 1, 3)
    pos = jnp.arange(T)
    nb = T // Q_BLOCK

    def blk(args):
        qc, tq = args
        s = jnp.einsum('bhqd,bhkd->bhqk', qc, kh)
        p = masked_softmax(s, tq[:, None] >= pos[None, :])
        return jnp.einsum('bhqk,bhkd->bhqd', p, vh)

    o = _from_chunks(lax.map(blk, (_to_chunks(qh, 2, nb), pos.reshape(nb, Q_BLOCK))), 2)
    return o.transpose(0, 2, 1, 3).reshape(B, T, MLA_OUT_W).astype(c_q.dtype)

def peer_ffn(x, w_query, sub_keys_1, sub_keys_2, expert_down, expert_up):
    f32 = jnp.float32
    B, T, D = x.shape
    H, K = PEER_HEADS, PEER_TOPK
    q = (x @ w_query).astype(f32).reshape(B, T, H, 2, PEER_QUERY_DIM // 2)
    s1 = jnp.einsum('bthd,nd->bthn', q[..., 0, :], sub_keys_1.astype(f32))
    s2 = jnp.einsum('bthd,nd->bthn', q[..., 1, :], sub_keys_2.astype(f32))
    v1, i1 = lax.top_k(s1, K)
    v2, i2 = lax.top_k(s2, K)
    cand_s = (v1[..., :, None] + v2[..., None, :]).reshape(B, T, H, K * K)
    cand_e = (i1[..., :, None] * PEER_N_KEYS + i2[..., None, :]).reshape(B, T, H, K * K)
    top_s, top_pos = lax.top_k(cand_s, K)
    experts = jnp.take_along_axis(cand_e, top_pos, axis=-1)
    g = jax.nn.softmax(top_s, axis=-1)
    n_tok = B * T
    c = math.gcd(n_tok, PEER_TOKEN_CHUNK)
    n_chunk = n_tok // c

    def expert_chunk(args):
        xt, e, gt = args
        u = expert_down[e].astype(f32)
        hdn = jax.nn.gelu(jnp.einsum('chkd,cd->chk', u, xt.astype(f32)))
        return jnp.einsum('chk,chkd->cd', gt * hdn, expert_up[e].astype(f32))

    y = lax.map(expert_chunk, (x.reshape(n_chunk, c, D), experts.reshape(n_chunk, c, H, K),
                               g.reshape(n_chunk, c, H, K)))
    return y.reshape(B, T, D).astype(x.dtype)

def setup_inputs(seed: int = 0) -> dict:
    key = jax.random.key(seed)
    ks = jax.random.split(key, 24)
    f32 = jnp.float32

    def nrm(k, shape, scale):
        return jax.random.normal(k, shape, f32) * scale

    def gain(k, n):
        return 1.0 + 0.02 * jax.random.normal(k, (DEPTH, n), f32)

    dk = NSA_HEAD_DIM
    return {
        'x': jax.random.normal(ks[0], (BATCH, SEQ, D_MODEL), f32),
        'positions': jnp.broadcast_to(jnp.arange(SEQ, dtype=jnp.int32)[None, :], (BATCH, SEQ)),
        'norm1_g': gain(ks[1], D_MODEL),
        'w_in': nrm(ks[2], (DEPTH, D_MODEL, IN_WIDTH), D_MODEL ** -0.5),
        'nsa_cmp_pos_k': nrm(ks[3], (DEPTH, CMP_BLOCK, dk), 0.1),
        'nsa_cmp_w1_k': nrm(ks[4], (DEPTH, CMP_BLOCK * dk, CMP_HIDDEN), (CMP_BLOCK * dk) ** -0.5),
        'nsa_cmp_w2_k': nrm(ks[5], (DEPTH, CMP_HIDDEN, dk), CMP_HIDDEN ** -0.5),
        'nsa_cmp_pos_v': nrm(ks[6], (DEPTH, CMP_BLOCK, dk), 0.1),
        'nsa_cmp_w1_v': nrm(ks[7], (DEPTH, CMP_BLOCK * dk, CMP_HIDDEN), (CMP_BLOCK * dk) ** -0.5),
        'nsa_cmp_w2_v': nrm(ks[8], (DEPTH, CMP_HIDDEN, dk), CMP_HIDDEN ** -0.5),
        'mla_q_norm_g': gain(ks[9], MLA_Q_LORA),
        'mla_kv_norm_g': gain(ks[10], MLA_KV_LORA),
        'mla_w_uq': nrm(ks[11], (DEPTH, MLA_Q_LORA, MLA_HEADS * (MLA_NOPE_DIM + MLA_ROPE_DIM)), MLA_Q_LORA ** -0.5),
        'mla_w_ukv': nrm(ks[12], (DEPTH, MLA_KV_LORA, MLA_HEADS * (MLA_NOPE_DIM + MLA_V_DIM)), MLA_KV_LORA ** -0.5),
        'w_branch_nsa': nrm(ks[13], (DEPTH, NSA_Q_W, D_MODEL), NSA_Q_W ** -0.5),
        'w_branch_mla': nrm(ks[14], (DEPTH, MLA_OUT_W, D_MODEL), MLA_OUT_W ** -0.5),
        'w_out': nrm(ks[15], (DEPTH, D_MODEL, D_MODEL), D_MODEL ** -0.5),
        'norm2_g': gain(ks[16], D_MODEL),
        'peer_w_query': nrm(ks[17], (DEPTH, D_MODEL, PEER_HEADS * PEER_QUERY_DIM), D_MODEL ** -0.5),
        'peer_sub_keys_1': nrm(ks[18], (DEPTH, PEER_N_KEYS, PEER_QUERY_DIM // 2), (PEER_QUERY_DIM // 2) ** -0.5),
        'peer_sub_keys_2': nrm(ks[19], (DEPTH, PEER_N_KEYS, PEER_QUERY_DIM // 2), (PEER_QUERY_DIM // 2) ** -0.5),
        'peer_expert_down': nrm(ks[20], (DEPTH, PEER_N_EXPERTS, D_MODEL), D_MODEL ** -0.5),
        'peer_expert_up': nrm(ks[21], (DEPTH, PEER_N_EXPERTS, D_MODEL), PEER_HEADS ** -0.5),
        'norm_f_g': 1.0 + 0.02 * jax.random.normal(ks[22], (D_MODEL,), f32),
    }

def reference(x, positions, norm1_g, w_in, nsa_cmp_pos_k, nsa_cmp_w1_k, nsa_cmp_w2_k,
              nsa_cmp_pos_v, nsa_cmp_w1_v, nsa_cmp_w2_v, mla_q_norm_g, mla_kv_norm_g,
              mla_w_uq, mla_w_ukv, w_branch_nsa, w_branch_mla, w_out, norm2_g,
              peer_w_query, peer_sub_keys_1, peer_sub_keys_2, peer_expert_down,
              peer_expert_up, norm_f_g):
    h = x
    for layer in range(DEPTH):
        xn = rms_norm(h, norm1_g[layer])
        (nsa_q, k_cmp, v_cmp, k_sel, v_sel, k_win, v_win, nsa_gates,
         mla_cq, mla_ckv, mla_kr, gate_nsa, gate_mla) = _split_columns(xn @ w_in[layer], IN_SPLITS)
        o_nsa = nsa_attention(nsa_q, k_cmp, v_cmp, k_sel, v_sel, k_win, v_win, nsa_gates,
                              nsa_cmp_pos_k[layer], nsa_cmp_w1_k[layer], nsa_cmp_w2_k[layer],
                              nsa_cmp_pos_v[layer], nsa_cmp_w1_v[layer], nsa_cmp_w2_v[layer])
        o_mla = mla_attention(mla_cq, mla_ckv, mla_kr, positions, mla_q_norm_g[layer],
                              mla_kv_norm_g[layer], mla_w_uq[layer], mla_w_ukv[layer])
        y_nsa = o_nsa @ w_branch_nsa[layer]
        y_mla = o_mla @ w_branch_mla[layer]
        merged = jax.nn.sigmoid(gate_nsa) * y_nsa + jax.nn.sigmoid(gate_mla) * y_mla
        h = h + merged @ w_out[layer]
        h = h + peer_ffn(rms_norm(h, norm2_g[layer]), peer_w_query[layer], peer_sub_keys_1[layer],
                         peer_sub_keys_2[layer], peer_expert_down[layer], peer_expert_up[layer])
    return rms_norm(h, norm_f_g)


_drawn_inputs = setup_inputs


def setup_inputs(seed=0):
    import zlib

    import numpy as np

    out = dict(_drawn_inputs(seed))
    spreads = {}
    factors = {'norm1_g': 3.342,
     'nsa_cmp_pos_k': 7.703,
     'mla_q_norm_g': 7.362,
     'mla_kv_norm_g': 5.149,
     'norm_f_g': 7.974,
     'nsa_cmp_pos_v': 7.017,
     'norm2_g': 7.704}
    for name, (base, spread) in spreads.items():
        noise = np.random.default_rng([zlib.crc32(name.encode()), seed]).standard_normal(out[name].shape)
        drawn = base * np.exp(spread * noise) if base else spread * noise
        out[name] = jnp.asarray(drawn.astype(out[name].dtype))
    for name, factor in factors.items():
        out[name] = (out[name] * factor).astype(out[name].dtype)
    return out
```

```python
from contextlib import ExitStack

import numpy as np

import concourse.bass as bass
from concourse import mybir

F32 = mybir.dt.float32
U32 = mybir.dt.uint32
I32 = mybir.dt.int32
ALU = mybir.AluOpType
ACT = mybir.ActivationFunctionType
AXX = mybir.AxisListType.X

P = 128
DM = 1024
TOK = 256
NT = TOK // P
KC = DM // P
HD = 64
NH = 8
NCMP = TOK // 16
ROPE = 32
QKW = HD + ROPE
NK = 128
TOP = 16
EPS = 1e-6
NEG = -1e30
LOWEST = -3e38
GELU_C = 0.044715
GELU_S = float(np.sqrt(2.0 / np.pi))
RING = 8
SLOTS = TOP
DVE_LINKS = 52
LOOPS = NH - 1

C_KCMP, C_VCMP, C_KSEL, C_VSEL, C_KWIN, C_VWIN, C_GATE, C_CQ, C_GN = (
    512, 640, 768, 896, 1024, 1152, 1280, 1304, 1720)
MLA_W = 416
CHUNKS = [(C_CQ, MLA_W), (C_KCMP, 512), (C_KWIN, 280), (0, 512)] + [(C_GN + 512 * c, 512) for c in range(4)]


class Steps:

    def __init__(self, eng, sem):
        self.eng, self.sem, self.n, self.turn = eng, sem, 0, 0

    def link(self, ins):
        ins.then_inc(self.sem, 1)
        self.n += 1
        self.eng.wait_ge(self.sem, self.turn + self.n)

    def mark(self, ins):
        ins.then_inc(self.sem, 1)
        self.n += 1

    def wait(self):
        self.eng.wait_ge(self.sem, self.turn + self.n)


def bc(ap, dims):
    return bass.AP(ap.tensor, ap.offset, [list(ap.ap[0])] + [list(d) for d in dims])


def block_program(nc, a, out):
    ctx = ExitStack()
    with ctx:
        def sb(name, words, dt=F32):
            return ctx.enter_context(nc.sbuf_tensor(name, [P, words], dt))

        def sem(name):
            return ctx.enter_context(nc.semaphore(name))

        region_q = sb("region_q", 16384)
        region_w = sb("region_w", 16384)
        x_sb = sb("x_sb", 2048)
        gates = sb("gates", 4096)
        xT = sb("xT", 2048)
        oT = sb("oT", 2048)
        g2b = sb("g2b", 1024)
        pool_bd = sb("pool_bd", 6400)
        ident = sb("ident", 128)
        skT = sb("skT", 256)
        g1c = sb("g1c", 8)
        gmc = sb("gmc", 3)
        stat = sb("stat", 64)
        io16 = sb("io16", 16)
        o_mla1 = sb("o_mla1", 512)

        banks = [ctx.enter_context(nc.psum_tensor(f"bank{i}", [P, 512], F32)) for i in range(8)]

        def view(t, at, *dims):
            n = int(np.prod(dims))
            v = t[:, at:at + n]
            if len(dims) == 2:
                return v.rearrange("p (a b) -> p a b", a=dims[0])
            if len(dims) == 3:
                return v.rearrange("p (a b c) -> p a b c", a=dims[0], b=dims[1])
            return v

        xs = view(x_sb, 0, 2, 1024)
        gt = view(gates, 0, 2, 2048)
        xTv = view(xT, 0, 8, 256)
        gfb = view(xT, 0, 1024)
        oTv = view(oT, 0, 8, 256)
        win = [view(region_q, 4096 * b, 4096) for b in range(2)]

        def chunk(c):
            return win[c % 2][:, 0:8 * CHUNKS[c][1]].rearrange("p (k n) -> p k n", k=KC)

        at = [8192]

        def in_q(*dims):
            v = view(region_q, at[0], *dims)
            at[0] += int(np.prod(dims))
            return v
        biasN = in_q(NH, 384)
        maskM = in_q(384)
        S_sb = [in_q(2, 256) for _ in range(2)]
        P_sb = [in_q(2, 256) for _ in range(2)]
        PT_sb = [in_q(512) for _ in range(2)]
        o_nsa = [in_q(512) for _ in range(2)]
        o_tmp = in_q(512)
        sk_in = o_tmp[:, 0:256]
        Sc = o_tmp[:, 256:512]
        assert at[0] <= 16384
        wq = view(region_q, 0, KC, 2048)
        wbn = view(region_w, 0, 4, 1024)
        wbm = view(region_w, 4096, 4, 1024)
        wo = view(region_w, 8192, KC, 1024)
        at[0] = 4096

        def in_w(*dims):
            v = view(region_w, at[0], *dims)
            at[0] += int(np.prod(dims))
            return v
        w_uqn, w_uqp = in_w(2, 512), in_w(2, 256)
        mlaT = in_w(3, 256)
        rope = in_w(2, 12, 32)
        w_uk, w_uv = in_w(512), in_w(512)
        w1 = [in_w(16, P) for _ in range(2)]
        kvc = [in_w(256) for _ in range(2)]
        kk = [[in_w(256) for _ in range(2)] for _ in range(2)]
        blk = [in_w(16, 32) for _ in range(2)]
        mla_tok = in_w(2, MLA_W)
        ropt = [in_w(12, 16) for _ in range(2)]
        trig = in_w(2, 2, 16)
        ang = in_w(5, 32)
        pos_row = in_w(2, 16)
        w2kd, w2v, hvrep = sb("w2kd", P)[:, :], sb("w2v", HD)[:, :], sb("hvrep", P)[:, :]
        cmpw = view(sb("cmpw", 320), 0, 5, 64)
        assert at[0] <= 16384
        ring_dn = view(region_w, 0, RING, 1024)
        ring_up = view(region_w, 8192, RING, 1024)
        at[0] = 0

        def in_b(*dims):
            v = view(pool_bd, at[0], *dims)
            at[0] += int(np.prod(dims))
            return v
        qT = in_b(4, 256)
        keyT = [in_b(256) for _ in range(2)]
        val = [in_b(2, P) for _ in range(2)]
        qnT = in_b(4, 256)
        knT = in_b(4, 256)
        vml = in_b(2, 512)
        peT = in_b(3, 256)
        VBD = in_b(512)
        nsag = sb("nsag", 48)
        kcT = sb("kcT", 32)
        biasC = sb("biasC", 256)
        maskC = sb("maskC", 32)
        blkmask = sb("blkmask", 8)
        PTc = sb("PTc", 256)
        coef = sb("coef", 64)
        sums = sb("sums", 56)
        mxs = sb("mxs", 8)
        assert at[0] <= 6400, at[0]
        at[0] = 0
        q_tok = [in_b(256) for _ in range(2)]
        q_T = [in_b(256) for _ in range(2)]
        top_v = in_b(2, TOP)
        top_if = in_b(2, TOP)
        scrap = in_b(256)
        cand = in_b(256)
        scrap2 = in_b(256)
        hot = in_b(256)
        hot2 = in_b(256)
        ts_v = in_b(TOP)
        ab_f = in_b(2, TOP)
        r12 = in_b(2, TOP)
        soft = [in_b(TOP) for _ in range(2)]
        hdn = in_b(TOP)
        gel = in_b(3, TOP)
        cof = [in_b(TOP) for _ in range(2)]
        diag = in_b(RING, P)
        d_stat = in_b(16)
        assert at[0] <= 6400
        top_i = sb("top_i", 32, U32)
        pos_i = sb("pos_i", 16, U32)
        ab_i = sb("ab_i", 32, U32)
        chosen = [sb(f"chosen{t}", TOP, U32) for t in range(2)]
        idx_dn = [sb(f"idx_dn{t}", TOP, U32) for t in range(2)]
        idx_up = [sb(f"idx_up{t}", TOP, U32) for t in range(2)]
        pos_i32 = sb("pos_i32", 2, I32)

        x_in = [sem(f"x_in{t}") for t in range(2)]
        win_in = [sem(f"win_in{b}") for b in range(2)]
        win_q_in = sem("win_q_in")
        win_used = sem("win_used")
        g1_in = sem("g1_in")
        vec_in, mla_w_in, cmp_w_in, g2_in, sk_sem, pos_in = (sem(n) for n in (
            "vec_in", "mla_w_in", "cmp_w_in", "g2_in", "sk_sem", "pos_in"))
        wbn_in, wbm_in, wo_in, wq_in, gf_in = (sem(n) for n in ("wbn_in", "wbm_in", "wo_in", "wq_in", "gf_in"))
        kk_in = sem("kk_in")
        id_ready, mask_ready, const_ready = sem("id_ready"), sem("mask_ready"), sem("const_ready")
        sk_mm, sk_cp = sem("sk_mm"), sem("sk_cp")
        rstd1, rstd_mla, rstd2, rstd3 = (sem(n) for n in ("rstd1", "rstd_mla", "rstd2", "rstd3"))
        ssq = sem("ssq")
        xn_ready = sem("xn_ready")
        xt_mm, xt_cp = sem("xt_mm"), sem("xt_cp")
        a_mm, a_cp = sem("a_mm"), sem("a_cp")
        ssq_mla, mla_scaled = sem("ssq_mla"), sem("mla_scaled")
        mt_mm, mt_cp = sem("mt_mm"), sem("mt_cp")
        j_mm = sem("j_mm")
        j_act, j_dve = sem("j_act"), sem("j_dve")
        ang_ready, trig_ready = sem("ang_ready"), sem("trig_ready")
        roped = sem("roped")
        pe_mm, pe_cp = sem("pe_mm"), sem("pe_cp")
        blk_ready = sem("blk_ready")
        hid_mm, hid_u, hid_t, hid_ready = sem("hid_mm"), sem("hid_u"), sem("hid_t"), sem("hid_ready")
        kc_mm, kc_cp, vbd_ready = sem("kc_mm"), sem("kc_cp"), sem("vbd_ready")
        sc_mm, sc_max, sc_exp, pc_ready = sem("sc_mm"), sem("sc_max"), sem("sc_exp"), sem("pc_ready")
        ptc_mm, ptc_cp, oc_mm, oc_done = sem("ptc_mm"), sem("ptc_cp"), sem("oc_mm"), sem("oc_done")
        s_mm, s_max, p_ready = sem("s_mm"), sem("s_max"), sem("p_ready")
        pt_mm, pt_cp, pv_mm, o_done = sem("pt_mm"), sem("pt_cp"), sem("pv_mm"), sem("o_done")
        ot_mm, ot_cp = sem("ot_mm"), sem("ot_cp")
        y_mm, y_used, merged = sem("y_mm"), sem("y_used"), sem("merged")
        mg_mm, mg_cp, wo_mm, h_ready = sem("mg_mm"), sem("mg_cp"), sem("wo_mm"), sem("h_ready")
        ssq2, xt2_ready, xt2_mm, xt2_cp = sem("ssq2"), sem("xt2_ready"), sem("xt2_mm"), sem("xt2_cp")
        q_mm, q_cp, qt_mm, qt_cp, key_mm = (sem(n) for n in ("q_mm", "q_cp", "qt_mm", "qt_cp", "key_mm"))
        keys_read, top_ready, exp_ready, soft_ready = (sem(n) for n in ("keys_read", "top_ready", "exp_ready", "soft_ready"))
        chosen_ready, chosen_taken = sem("chosen_ready"), sem("chosen_taken")
        dn_in = [sem(f"dn_in{r}") for r in range(RING)]
        up_in = [sem(f"up_in{r}") for r in range(RING)]
        dn_used, up_used = sem("dn_used"), sem("up_used")
        poly_ready, tanh_ready, cof_ready, diag_ready = (sem(n) for n in ("poly_ready", "tanh_ready", "cof_ready", "diag_ready"))
        y_zero, y_started, y_done = sem("y_zero"), sem("y_started"), sem("y_done")
        hy_ready, ssq3, out_ready, out_sem = sem("hy_ready"), sem("ssq3"), sem("out_ready"), sem("out_sem")
        pass_pool = sem("pass_pool")
        pass_dve = sem("pass_dve")
        own_pe = sem("own_pe")
        own_dve, own_act, own_pool = sem("own_dve"), sem("own_act"), sem("own_pool")

        UNITS = [(kind, t, j) for kind in ("sel", "win", "mla") for t in range(2) for j in range(4)]

        def heads(kind, j):
            return (2 * j, 2 * j + 1) if kind == "mla" else (j, 4 + j)

        GATE_MM = 4 * NT * KC

        GATE_HID, GATE_CMP, GATE_PRE = 8, 16, 20

        def gate_upto(n):
            return GATE_PRE + (GATE_MM - GATE_PRE) * (n + 1) // len(UNITS)

        def gate_tanh(act, v):
            c, t = v // 2, v % 2
            act.wait_ge(a_mm, 14 + v + 1)
            act.activation(gt[:, t, 512 * c:512 * (c + 1)], banks[6 + v % 2][:, :], ACT.Tanh, scale=0.5).then_inc(a_cp, 1)

        def view_trig_in(v):
            return v[:, 3:5, :].rearrange("p c (t f) -> p c t f", t=2)

        def mg_bank(t, half):
            return ((4, 5), (7, 2))[t][half]

        def xt2_bank(t, half):
            return ((4, 5), (7, 3))[t][half]

        def wo_bank(t, half):
            return 2 * (1 - t) + half

        def y_bank(t, n):
            return ((4, 5, 6, 7), (0, 1, 6, 7))[t][n]

        w_in = a["w_in"]
        tok_rows = [slice(t * P, (t + 1) * P) for t in range(2)]

        block = ctx.enter_context(nc.Block())

        @block.sync
        def _(sp):
            def load_chunk(c):
                c0, n = CHUNKS[c]
                if c >= 2:
                    sp.wait_ge(win_used, c - 1)
                if c != 3:
                    sp.dma_start(chunk(c), w_in[:, c0:c0 + n].rearrange("(k p) n -> p k n", p=P)).then_inc(win_in[c % 2], 16)
                    return
                pairs = chunk(c).rearrange("p k (j g c) -> p k j g c", j=4, g=2)
                for g in range(2):
                    for k in range(KC):
                        sp.dma_start(pairs[:, k, :, g, :], w_in[k * P:(k + 1) * P, 256 * g:256 * (g + 1)].rearrange(
                            "p (j c) -> p j c", j=4)).then_inc(win_q_in, 16)

            for t in range(2):
                sp.dma_start(xs[:, t, :], a["x"][tok_rows[t], :]).then_inc(x_in[t], 16)
            load_chunk(0)
            load_chunk(1)
            uq = a["w_uq"].rearrange("(k p) (h c) -> p k h c", p=P, h=NH)
            ukv = a["w_ukv"].rearrange("p (h c) -> p h c", h=NH)
            for k in range(2):
                sp.dma_start(w_uqn[:, k, :].rearrange("p (h c) -> p h c", h=NH), uq[:, k, :, 0:HD]).then_inc(mla_w_in, 16)
                sp.dma_start(w_uqp[:, k, :].rearrange("p (h c) -> p h c", h=NH), uq[:, k, :, HD:QKW]).then_inc(mla_w_in, 16)
            sp.dma_start(w_uk.rearrange("p (h c) -> p h c", h=NH), ukv[:, :, 0:HD]).then_inc(mla_w_in, 16)
            sp.dma_start(w_uv.rearrange("p (h c) -> p h c", h=NH), ukv[:, :, HD:2 * HD]).then_inc(mla_w_in, 16)
            for v, name in enumerate(("w1k", "w1v")):
                sp.dma_start(w1[v], a[name].rearrange("(l p) n -> p l n", p=P)).then_inc(cmp_w_in, 16)
            for c in range(2):
                sp.dma_start(w2kd[:, c * HD:(c + 1) * HD], a["w2k"]).then_inc(cmp_w_in, 16)
            sp.dma_start(w2v, a["w2v"]).then_inc(cmp_w_in, 16)
            load_chunk(2)
            for v in range(2):
                sp.wait_ge(a_cp, 3 + v)
                for g in range(2):
                    rows = slice(g * HD, (g + 1) * HD)
                    sp.dma_start(kk[v][g][0:HD, :], kvc[v][rows, :]).then_inc(kk_in, 16)
                    sp.dma_start(kk[v][g][HD:P, 0:TOK - 1], kvc[v][rows, 1:TOK]).then_inc(kk_in, 16)
            load_chunk(3)
            for c in range(4, 8):
                load_chunk(c)
                if c == 5:
                    sp.dma_start(wbn, a["wb_nsa"].rearrange("(k p) n -> p k n", p=P)).then_inc(wbn_in, 16)
            sp.wait_ge(pe_cp, 2)
            sp.wait_ge(vbd_ready, 1)
            sp.wait_ge(kc_cp, 1)
            sp.dma_start(wbm, a["wb_mla"].rearrange("(k p) n -> p k n", p=P)).then_inc(wbm_in, 16)
            sp.dma_start(wo, a["w_out"].rearrange("(k p) n -> p k n", p=P)).then_inc(wo_in, 16)
            sp.wait_ge(ot_cp, 4)
            sp.wait_ge(win_used, 8)
            sp.dma_start(wq, a["w_query"].rearrange("(k p) n -> p k n", p=P)).then_inc(wq_in, 16)
            sp.wait_ge(wo_mm, 4)
            sp.dma_start(gfb, a["norm_f_g"].rearrange("(o n) -> o n", o=1).broadcast_to([P, DM])).then_inc(gf_in, 16)
            for t in range(2):
                sp.wait_ge(out_ready, t + 1)
                sp.dma_start(out[tok_rows[t], :], x_sb[:, t * DM:(t + 1) * DM]).then_inc(out_sem, 16)
            sp.wait_ge(out_sem, 32)

        @block.gpsimd
        def _(pool):
            own = Steps(pool, own_pool)
            pool.dma_start(g1c[:, :], a["norm1_g"].rearrange("o (k p) -> p (o k)", p=P), allow_slow_non_contiguous=True).then_inc(g1_in, 16)
            pool.dma_start(g2b[:, :], a["norm2_g"].broadcast_to([P, DM])).then_inc(g2_in, 16)

            own.link(pool.memset(ident[:, :], 0.0))
            pool.affine_select(out=ident[:, :], in_=ident[:, :], compare_op=ALU.not_equal, fill=1.0, base=0,
                               pattern=[[-1, P]], channel_multiplier=1).then_inc(id_ready, 1)
            def rstd(dst, src, n):
                own.link(pool.tensor_scalar(out=dst, in0=src, scalar1=1.0 / n, scalar2=EPS, op0=ALU.mult, op1=ALU.add))
                return pool.tensor_tensor(out=dst, in0=dst, in1=stat[:, 63:64], op=ALU.pow)

            own.link(pool.memset(stat[:, 63:64], -0.5))

            for t in range(2):
                pool.wait_ge(ssq, t + 1)
                rstd(stat[:, 2 + t:3 + t], stat[:, t:t + 1], DM).then_inc(rstd1, 1)
            for j in range(16):
                pool.memset(ang[:, 0, j:j + 1], float(np.float32(10000.0) ** np.float32(-2.0 * j / ROPE)))
            own.link(pool.iota(io16[:, :], [[1, 16]], base=0, channel_multiplier=0, allow_small_or_imprecise_dtypes=True))
            pool.engine_nop().then_inc(const_ready, 1)
            for v in range(2):
                pool.memset(blk[v][:, :, :], 0.0)
            own.link(pool.memset(maskM, 0.0))
            for t in range(2):
                cols = maskM[:, t * P:t * P + (t + 1) * P]
                own.link(pool.affine_select(out=cols, in_=cols, compare_op=ALU.is_ge, fill=NEG, base=t * P,
                                            pattern=[[-1, (t + 1) * P]], channel_multiplier=1))
            for t in range(2):
                n = (t + 1) * P
                own.link(pool.iota(biasN[:, 0, t * P:t * P + n], [[-1, n]], base=t * P, channel_multiplier=1,
                                   allow_small_or_imprecise_dtypes=True))
            for h in range(NH - 1, -1, -1):
                own.link(pool.tensor_scalar(out=biasN[:, h, :], in0=biasN[:, 0, :], scalar1=-(2.0 ** -(h + 1)), scalar2=None, op0=ALU.mult))
                for t in range(2):
                    cols = biasN[:, h, t * P:t * P + (t + 1) * P]
                    pool.affine_select(out=cols, in_=cols, compare_op=ALU.is_ge, fill=NEG, base=t * P,
                                       pattern=[[-1, (t + 1) * P]], channel_multiplier=1).then_inc(mask_ready, 1)
            for t in range(2):
                for part, width in enumerate((256, 128)):
                    pool.wait_ge(ssq_mla, 2 * t + part + 1)
                    rstd(stat[:, 8 + 2 * t + part:9 + 2 * t + part], stat[:, 4 + 2 * t + part:5 + 2 * t + part], width).then_inc(rstd_mla, 1)
            own.link(pool.memset(maskC[:, :], 1.0))
            for t in range(2):
                cols = maskC[:, t * 16:(t + 1) * 16]
                own.link(pool.affine_select(out=cols, in_=cols, compare_op=ALU.is_ge, fill=0.0, base=t * P - 31,
                                            pattern=[[-16, 16]], channel_multiplier=1))
                own.link(pool.iota(biasC[:, t * P:t * P + 16], [[-16, 16]], base=t * P - 31, channel_multiplier=1,
                                   allow_small_or_imprecise_dtypes=True))
                for h in range(NH - 1, -1, -1):
                    cols = biasC[:, t * P + h * 16:t * P + (h + 1) * 16]
                    own.link(pool.tensor_scalar(out=cols, in0=biasC[:, t * P:t * P + 16], scalar1=-(2.0 ** -(h + 1)), scalar2=None, op0=ALU.mult))
                    own.link(pool.affine_select(out=cols, in_=cols, compare_op=ALU.is_ge, fill=NEG, base=t * P - 31,
                                                pattern=[[-16, 16]], channel_multiplier=1))
            own.link(pool.memset(blkmask[:, :], 1.0))
            own.link(pool.affine_select(out=blkmask[:, :], in_=blkmask[:, :], compare_op=ALU.is_ge, fill=0.0, base=0,
                                        pattern=[[-16, 8]], channel_multiplier=1))
            own.link(pool.affine_select(out=blkmask[:, :], in_=blkmask[:, :], compare_op=ALU.is_ge, fill=0.0, base=15,
                                        pattern=[[16, 8]], channel_multiplier=-1))
            pool.engine_nop().then_inc(mask_ready, 1)

            def rstd_h(t):
                pool.wait_ge(ssq2, t + 1)
                rstd(stat[:, 18 + t:19 + t], stat[:, 16 + t:17 + t], DM).then_inc(rstd2, 1)

            rstd_h(0)

            def take(t, s):
                pool.wait_ge(chosen_ready, s + 1)
                pool.sem_inc(pass_pool, 1)
                pool.tensor_copy(idx_dn[t][:, :], chosen[t][:, :]).then_inc(chosen_taken, 1)
                pool.wait_ge(chosen_taken, s + 1)
                pool.sem_inc(pass_pool, 1)

            def keep(t):
                own.link(pool.tensor_copy(idx_up[t][:, :], idx_dn[t][:, :]))
                pool.sem_inc(pass_pool, 1)

            def gather(ring, arrived, used, table, idx, k, s, first):
                if not (first and k < RING):
                    pool.wait_ge(used, s * SLOTS + k - RING + 1)
                    pool.sem_inc(pass_pool, 1)
                pool.indirect_dma_start(
                    out=ring[:, k % RING, :], out_offset=None, in_=table,
                    in_offset=bass.IndirectOffsetOnAxis(ap=idx[:, k:k + 1], axis=0)).then_inc(arrived[k % RING], 16)

            def down(t, k, s, first=False):
                gather(ring_dn, dn_in, dn_used, a["expert_down"], idx_dn[t], k, s, first)

            def up(t, k, s, first=False):
                gather(ring_up, up_in, up_used, a["expert_up"], idx_up[t], k, s, first)

            pool.wait_ge(y_mm, 8)
            take(0, 0)
            for k in range(SLOTS):
                if k == RING // 2:
                    rstd_h(1)
                down(0, k, 0, first=True)
            pool.wait_ge(wo_mm, 4)
            keep(0)
            for k in range(RING):
                up(0, k, 0, first=True)
            take(1, 1)
            for k in range(SLOTS):
                down(1, k, 1)
                if k < SLOTS - RING:
                    up(0, k + RING, 0)
            keep(1)
            take(0, 2)
            for k in range(SLOTS):
                down(0, k, 2)
                up(1, k, 1)
            n0 = own.n
            with pool.Fori(1, LOOPS) as i:
                own.turn = (i - 1) * 2
                own.n = n0
                keep(0)
                take(1, 2 * i + 1)
                for k in range(SLOTS):
                    down(1, k, 2 * i + 1)
                    up(0, k, 2 * i)
                keep(1)
                take(0, 2 * i + 2)
                for k in range(SLOTS):
                    down(0, k, 2 * i + 2)
                    up(1, k, 2 * i + 1)
            own.turn, own.n = 0, n0 + 2 * (LOOPS - 1)
            keep(0)
            take(1, 2 * LOOPS + 1)
            for k in range(SLOTS):
                down(1, k, 2 * LOOPS + 1)
                up(0, k, 2 * LOOPS)
            keep(1)
            for k in range(SLOTS):
                up(1, k, 2 * LOOPS + 1)
            for t in range(2):
                pool.wait_ge(ssq3, t + 1)
                rstd(stat[:, 26 + t:27 + t], stat[:, 24 + t:25 + t], DM).then_inc(rstd3, 1)

        @block.scalar
        def _(act):
            own = Steps(act, own_act)

            def copy(out_, in_, scale=1.0):
                return act.activation(out_, in_, ACT.Copy, scale=scale)

            for t in range(2):
                act.wait_ge(x_in[t], 16)
                act.activation(xTv[:, 4 * t:4 * t + 4, :], xs[:, t, :].rearrange("p (a b) -> p a b", a=4), ACT.Square,
                               accum_out=stat[:, t:t + 1]).then_inc(ssq, 1)
            act.dma_start(gmc[:, 0:2], a["mla_q_norm_g"].rearrange("o (k p) -> p (o k)", p=P), allow_slow_non_contiguous=True).then_inc(vec_in, 16)
            act.dma_start(gmc[:, 2:3], a["mla_kv_norm_g"].rearrange("o (k p) -> p (o k)", p=P), allow_slow_non_contiguous=True).then_inc(vec_in, 16)
            act.dma_start(pos_i32[:, :], a["positions"].rearrange("o (t p) -> p (o t)", p=P), allow_slow_non_contiguous=True).then_inc(pos_in, 16)
            for n, name in enumerate(("sub_keys_1", "sub_keys_2")):
                act.dma_start(sk_in[:, n * P:(n + 1) * P], a[name]).then_inc(sk_sem, 16)
            for v, name in enumerate(("pos_k", "pos_v")):
                for half in range(2):
                    act.dma_start(pos_row[half * HD:(half + 1) * HD, v, :],
                                   a[name].rearrange("(l h) d -> h d l", h=2)[half], allow_slow_non_contiguous=True).then_inc(pos_in, 16)
            def a_unit(u, dst, cols=None, scale=1.0):
                act.wait_ge(a_mm, u + 1)
                w = cols or dst.shape[-1]
                return copy(dst, banks[6 + u % 2][:, 0:w], scale)

            for t in range(2):
                a_unit(t, mla_tok[:, t, :]).then_inc(a_cp, 1)
            act.wait_ge(a_cp, 2)
            for t in range(2):
                act.activation(rope[:, t, 0:8, :], mla_tok[:, t, 0:256].rearrange("p (a b) -> p a b", a=8), ACT.Square,
                               accum_out=stat[:, 4 + 2 * t:5 + 2 * t]).then_inc(ssq_mla, 1)
                act.activation(rope[:, t, 8:12, :], mla_tok[:, t, 256:384].rearrange("p (a b) -> p a b", a=4), ACT.Square,
                               accum_out=stat[:, 5 + 2 * t:6 + 2 * t]).then_inc(ssq_mla, 1)
            a_unit(2, kvc[0]).then_inc(a_cp, 1)
            a_unit(3, kvc[1]).then_inc(a_cp, 1)
            a_unit(4, keyT[0]).then_inc(a_cp, 1)
            for t in range(2):
                a_unit(5 + t, val[0][:, t, :]).then_inc(a_cp, 1)
            a_unit(7, keyT[1]).then_inc(a_cp, 1)
            for t in range(2):
                a_unit(8 + t, val[1][:, t, :], P)
                act.activation(nsag[:, t * 24:(t + 1) * 24], banks[6 + (8 + t) % 2][:, P:P + 24], ACT.Tanh, scale=0.5).then_inc(a_cp, 1)
            act.wait_ge(ang_ready, 1)
            act.activation(trig[:, :, :, :], view_trig_in(ang), ACT.Sin).then_inc(trig_ready, 1)
            act.wait_ge(sk_mm, 1)
            copy(skT[:, :], banks[0][:, 0:256]).then_inc(sk_cp, 1)

            mla_scale = float(np.float32(QKW ** -0.5))
            for b in range(2):
                act.wait_ge(j_mm, b + 1)
                copy(qnT[:, 2 * b:2 * b + 2, :], banks[b][:, :].rearrange("p (a b) -> p a b", a=2), mla_scale).then_inc(j_act, 1)
            for n, b in enumerate((5, 2)):
                act.wait_ge(j_mm, 4 + n)
                copy(knT[:, 2 * n:2 * n + 2, :], banks[b][:, :].rearrange("p (a b) -> p a b", a=2)).then_inc(j_act, 1)
            for j in range(4):
                a_unit(10 + j, qT[:, j, :], scale=HD ** -0.5).then_inc(a_cp, 1)
            for t, b in enumerate((1, 4)):
                act.wait_ge(pe_mm, t + 1)
                src = banks[b][:, 0:384].rearrange("p (a b) -> p a b", a=3)
                copy(peT[:, 0:2, tok_rows[t]], src[:, 0:2, :], mla_scale)
                copy(peT[:, 2, tok_rows[t]], src[:, 2, :]).then_inc(pe_cp, 1)
            act.wait_ge(hid_u, 1)
            act.activation(cmpw[:, 2, :], cmpw[:, 1, :], ACT.Tanh, scale=GELU_S).then_inc(hid_t, 1)
            gate_tanh(act, 0)
            act.wait_ge(kc_mm, 2)
            copy(kcT[:, :], banks[2][:, 0:32]).then_inc(kc_cp, 1)
            for t in range(2):
                act.wait_ge(sc_max, t + 1)
                act.activation(Sc[:, t * P:(t + 1) * P], Sc[:, t * P:(t + 1) * P], ACT.Exp).then_inc(sc_exp, 1)
            gate_tanh(act, 1)
            done = 2
            for n, (kind, t, j) in enumerate(UNITS):
                act.wait_ge(s_max, n + 1)
                if n >= 2:
                    act.wait_ge(pt_mm, n - 1)
                K = (t + 1) * P
                for e, h in enumerate(heads(kind, j)):
                    at_sum = (n // 4) * 8 + h
                    act.activation(P_sb[n % 2][:, e, 0:K], S_sb[n % 2][:, e, 0:K], ACT.Exp,
                                   bias=mxs[:, 4 * (n % 2) + 2 + e:4 * (n % 2) + 3 + e],
                                   accum_out=sums[:, at_sum:at_sum + 1]).then_inc(p_ready, 1)
                while KC * (done + 1) <= gate_upto(n - 1):
                    gate_tanh(act, done)
                    done += 1
            while done < 8:
                gate_tanh(act, done)
                done += 1
            for b in range(4):
                act.wait_ge(ot_mm, b + 1)
                t, part = b % 2, b // 2
                copy(oTv[:, 4 * part:4 * part + 4, tok_rows[t]], banks[b][:, :].rearrange("p (a b) -> p a b", a=4)).then_inc(ot_cp, 1)
            def mergedT_copy(t):
                for half in range(2):
                    act.wait_ge(mg_mm, 2 * t + half + 1)
                    copy(xTv[:, 4 * half:4 * half + 4, tok_rows[t]],
                         banks[mg_bank(t, half)][:, :].rearrange("p (a b) -> p a b", a=4)).then_inc(mg_cp, 1)

            def square_h(t):
                act.wait_ge(h_ready, t + 1)
                act.activation(gt[:, t, DM:2 * DM], xs[:, t, :], ACT.Square, accum_out=stat[:, 16 + t:17 + t]).then_inc(ssq2, 1)

            def normedT_copy(t):
                for half in range(2):
                    act.wait_ge(xt2_mm, 2 * t + half + 1)
                    copy(oTv[:, 4 * half:4 * half + 4, tok_rows[t]],
                         banks[xt2_bank(t, half)][:, :].rearrange("p (a b) -> p a b", a=4)).then_inc(xt2_cp, 1)

            def query_copy(t, p):
                act.wait_ge(q_mm, p + 1)
                copy(q_tok[t], banks[4][:, t * 256:(t + 1) * 256]).then_inc(q_cp, 1)

            def queryT_copy(t, p):
                act.wait_ge(qt_mm, p + 1)
                copy(q_T[t], banks[5][:, t * 256:(t + 1) * 256]).then_inc(qt_cp, 1)

            def softmax_exp(t, p):
                act.wait_ge(top_ready, p + 1)
                act.activation(soft[t], ts_v, ACT.Exp, bias=d_stat[:, 0:1], accum_out=d_stat[:, 1:2]).then_inc(exp_ready, 1)

            def gelu_tanh(s):
                act.wait_ge(poly_ready, s + 1)
                act.activation(gel[:, 1, :], gel[:, 0, :], ACT.Tanh, scale=GELU_S).then_inc(tanh_ready, 1)

            def diagonal(t, k, s, first=False):
                if k == 0:
                    act.wait_ge(cof_ready, s + 1)
                if not (first and k < RING):
                    act.wait_ge(up_used, s * SLOTS + k - RING + 1)
                act.activation(diag[:, k % RING, :], ident[:, :], ACT.Copy, scale=cof[t][:, k:k + 1]).then_inc(diag_ready, 1)

            def half_step(t_up, s, prepare, dots, first=False):
                if prepare:
                    query_copy(t_up, s + 2)
                for k in range(SLOTS):
                    if k == 4 and prepare:
                        queryT_copy(t_up, s + 2)
                    if k == 12 and prepare:
                        softmax_exp(t_up, s + 2)
                    diagonal(t_up, k, s, first)
                if dots:
                    gelu_tanh(s + 1)

            mergedT_copy(0)
            square_h(0)
            normedT_copy(0)
            query_copy(0, 0)
            mergedT_copy(1)
            queryT_copy(0, 0)
            softmax_exp(0, 0)
            square_h(1)
            normedT_copy(1)
            query_copy(1, 1)
            queryT_copy(1, 1)
            softmax_exp(1, 1)
            gelu_tanh(0)
            act.wait_ge(y_started, 1)
            half_step(0, 0, True, True, first=True)
            half_step(1, 1, True, True)
            with act.Fori(1, LOOPS) as i:
                half_step(0, 2 * i, True, True)
                half_step(1, 2 * i + 1, True, True)
            half_step(0, 2 * LOOPS, False, True)
            half_step(1, 2 * LOOPS + 1, False, False)
            for t in range(2):
                act.wait_ge(hy_ready, t + 1)
                act.activation(gt[:, t, 0:DM], xs[:, t, :], ACT.Square, accum_out=stat[:, 24 + t:25 + t]).then_inc(ssq3, 1)

        @block.vector
        def _(dve):
            own = Steps(dve, own_dve)
            link = own.link

            for t in range(2):
                dve.wait_ge(rstd1, t + 1)
                dve.tensor_scalar(out=gt[:, t, 0:DM], in0=xs[:, t, :], scalar1=stat[:, 2 + t:3 + t], scalar2=None, op0=ALU.mult).then_inc(xn_ready, 1)
            dve.wait_ge(g1_in, 16)
            for n in range(4):
                t, half = n // 2, n % 2
                dve.wait_ge(xt_mm, n + 1)
                dve.tensor_tensor(out=xTv[:, 4 * half:4 * half + 4, tok_rows[t]],
                                  in0=banks[2 + n % 2][:, :].rearrange("p (a b) -> p a b", a=4),
                                  in1=bc(g1c[:, 4 * half:4 * half + 1], [[1, 4], [0, P]]), op=ALU.mult).then_inc(xt_cp, 1)
            dve.wait_ge(pos_in, 80)
            dve.wait_ge(const_ready, 1)
            link(dve.tensor_copy(stat[:, 30:32], pos_i32[:, :]))
            for t in range(2):
                dve.tensor_scalar(out=ang[:, 4, 16 * t:16 * t + 16], in0=ang[:, 0, 0:16], scalar1=stat[:, 30 + t:31 + t],
                                  scalar2=None, op0=ALU.mult).then_inc(own_dve, 1)
            own.n += 2
            dve.wait_ge(own_dve, own.n)
            two_pi = 2.0 * np.pi
            c1 = 6.28125
            c2 = float(np.float32(two_pi - c1))
            c3 = float(two_pi - c1 - c2)
            magic = 12582912.0
            link(dve.tensor_scalar(out=ang[:, 1, :], in0=ang[:, 4, :], scalar1=float(1.0 / two_pi), scalar2=None, op0=ALU.mult))
            link(dve.tensor_scalar(out=ang[:, 1, :], in0=ang[:, 1, :], scalar1=magic, scalar2=None, op0=ALU.add))
            link(dve.tensor_scalar(out=ang[:, 1, :], in0=ang[:, 1, :], scalar1=magic, scalar2=None, op0=ALU.subtract))
            for c in (c1, c2, c3):
                link(dve.scalar_tensor_tensor(out=ang[:, 4, :], in0=ang[:, 1, :], scalar=-c, in1=ang[:, 4, :], op0=ALU.mult, op1=ALU.add))
            link(dve.tensor_scalar(out=ang[:, 3, :], in0=ang[:, 4, :], scalar1=float(np.pi / 2), scalar2=None, op0=ALU.add))
            link(dve.tensor_scalar(out=ang[:, 2, :], in0=ang[:, 3, :], scalar1=float(np.pi), scalar2=two_pi, op0=ALU.is_gt, op1=ALU.mult))
            link(dve.tensor_tensor(out=ang[:, 3, :], in0=ang[:, 3, :], in1=ang[:, 2, :], op=ALU.subtract))
            dve.tensor_scalar(out=ang[:, 3:5, :], in0=ang[:, 3:5, :], scalar1=3.1415925, scalar2=-3.1415925, op0=ALU.min, op1=ALU.max).then_inc(ang_ready, 1)

            for t in range(2):
                dve.wait_ge(rstd_mla, 2 * t + 2)
                dve.tensor_scalar(out=mla_tok[:, t, 0:256], in0=mla_tok[:, t, 0:256], scalar1=stat[:, 8 + 2 * t:9 + 2 * t],
                                  scalar2=None, op0=ALU.mult).then_inc(mla_scaled, 1)
                dve.tensor_scalar(out=mla_tok[:, t, 256:384], in0=mla_tok[:, t, 256:384], scalar1=stat[:, 9 + 2 * t:10 + 2 * t],
                                  scalar2=None, op0=ALU.mult).then_inc(mla_scaled, 1)
            dve.wait_ge(vec_in, 32)
            for t in range(2):
                dve.wait_ge(mt_mm, t + 1)
                dve.tensor_tensor(out=mlaT[:, :, tok_rows[t]], in0=banks[2 + t][:, 0:384].rearrange("p (a b) -> p a b", a=3),
                                  in1=bc(gmc[:, 0:1], [[1, 3], [0, P]]), op=ALU.mult).then_inc(mt_cp, 1)
            dve.wait_ge(kk_in, 8 * 16)
            dve.wait_ge(mask_ready, 17)
            for v in range(2):
                for g in range(2):
                    dve.tensor_tensor(out=blk[v][:, :, 16 * g:16 * g + 15],
                                      in0=bc(kk[v][g][:, 0:1], [[2, 16], [16, 15]]),
                                      in1=bc(pos_row[:, v, 0:1], [[1, 16], [0, 15]]), op=ALU.add).then_inc(blk_ready, 1)
            dve.wait_ge(trig_ready, 1)
            dve.wait_ge(j_mm, 3)
            dve.wait_ge(ssq_mla, 4)
            for t in range(2):
                src = bc(mla_tok[:, t, 384:385], [[0, 4], [1, ROPE]])
                dve.tensor_copy(rope[:, t, 0:8, :], banks[4][:, 256 * t:256 * t + 256].rearrange("p (a b) -> p a b", a=8)).then_inc(own_dve, 1)
                dve.tensor_copy(rope[:, t, 8:12, :], src).then_inc(own_dve, 1)
                own.n += 2
                dve.wait_ge(own_dve, own.n)
                x1, x2 = rope[:, t, :, 0:16], rope[:, t, :, 16:32]
                cos = bc(trig[:, 0, t, 0:1], [[0, 12], [1, 16]])
                sin = bc(trig[:, 1, t, 0:1], [[0, 12], [1, 16]])
                dve.tensor_tensor(out=ropt[0], in0=x1, in1=sin, op=ALU.mult).then_inc(own_dve, 1)
                dve.tensor_tensor(out=ropt[1], in0=x2, in1=sin, op=ALU.mult).then_inc(own_dve, 1)
                own.n += 2
                dve.wait_ge(own_dve, own.n)
                link(dve.tensor_tensor(out=x1, in0=x1, in1=cos, op=ALU.mult))
                link(dve.tensor_tensor(out=x2, in0=x2, in1=cos, op=ALU.mult))
                dve.tensor_tensor(out=x1, in0=x1, in1=ropt[1], op=ALU.subtract).then_inc(own_dve, 1)
                dve.tensor_tensor(out=x2, in0=x2, in1=ropt[0], op=ALU.add).then_inc(own_dve, 1)
                own.n += 2
                dve.wait_ge(own_dve, own.n)
                dve.engine_nop().then_inc(roped, 1)
            for t, b in enumerate((3, 0)):
                dve.wait_ge(j_mm, 6 + t)
                dve.tensor_copy(vml[:, t, :], banks[b][:, :]).then_inc(j_dve, 1)
            dve.wait_ge(hid_mm, 1)
            link(dve.tensor_copy(cmpw[:, 0, :], banks[5][:, 0:64]))
            link(dve.tensor_tensor(out=cmpw[:, 1, :], in0=cmpw[:, 0, :], in1=cmpw[:, 0, :], op=ALU.mult))
            link(dve.tensor_scalar(out=cmpw[:, 1, :], in0=cmpw[:, 1, :], scalar1=GELU_C, scalar2=1.0, op0=ALU.mult, op1=ALU.add))
            dve.tensor_tensor(out=cmpw[:, 1, :], in0=cmpw[:, 1, :], in1=cmpw[:, 0, :], op=ALU.mult).then_inc(hid_u, 1)
            dve.wait_ge(hid_t, 1)
            link(dve.scalar_tensor_tensor(out=cmpw[:, 3, :], in0=cmpw[:, 2, :], scalar=1.0, in1=cmpw[:, 0, :], op0=ALU.add, op1=ALU.mult))
            link(dve.tensor_scalar(out=cmpw[:, 4, :], in0=cmpw[:, 3, :], scalar1=0.5, scalar2=None, op0=ALU.mult))
            dve.tensor_copy(hvrep.rearrange("p (g j n) -> p g j n", g=2, j=4),
                            bc(cmpw[:, 4, 32:33], [[16, 2], [0, 4], [1, 16]])).then_inc(hid_ready, 1)
            dve.wait_ge(kc_cp, 1)
            dve.tensor_tensor(out=VBD.rearrange("p (h d) -> p h d", h=NH), in0=bc(banks[2][:, 64:65], [[0, NH], [1, HD]]),
                              in1=bc(blkmask[:, 0:1], [[1, NH], [0, HD]]), op=ALU.mult).then_inc(vbd_ready, 1)
            dve.wait_ge(a_cp, 10)
            link(dve.tensor_scalar(out=nsag[:, :], in0=nsag[:, :], scalar1=0.5, scalar2=0.5, op0=ALU.mult, op1=ALU.add))

            def heads_scaled(dst, src, scal):
                return dve.tensor_tensor(out=dst.rearrange("p (h d) -> p h d", h=NH), in0=src.rearrange("p (h d) -> p h d", h=NH),
                                         in1=bc(scal, [[1, NH], [0, HD]]), op=ALU.mult)

            for t in range(2):
                sc = Sc[:, t * P:(t + 1) * P]
                sc3 = sc.rearrange("p (h n) -> p h n", h=NH)
                dve.wait_ge(sc_mm, t + 1)
                link(dve.tensor_tensor(out=sc, in0=banks[t][:, 0:P], in1=biasC[:, t * P:(t + 1) * P], op=ALU.add))
                link(dve.tensor_reduce(out=coef[:, 32:40], in_=sc3, axis=AXX, op=ALU.max))
                dve.tensor_tensor(out=sc3, in0=sc3, in1=bc(coef[:, 32:33], [[1, NH], [0, 16]]), op=ALU.subtract).then_inc(sc_max, 1)
                dve.wait_ge(sc_max, t + 1)
            for t in range(2):
                sc3 = Sc[:, t * P:(t + 1) * P].rearrange("p (h n) -> p h n", h=NH)
                dve.wait_ge(sc_exp, t + 1)
                link(dve.tensor_tensor(out=sc3, in0=sc3, in1=bc(maskC[:, 16 * t:16 * t + 1], [[0, NH], [1, 16]]), op=ALU.mult))
                dve.engine_nop().then_inc(pc_ready, 1)
                cc = coef[:, 8 * t:8 * t + 8]
                link(dve.tensor_reduce(out=cc, in_=sc3, axis=AXX, op=ALU.add))
                link(dve.tensor_scalar(out=cc, in0=cc, scalar1=1e-30, scalar2=None, op0=ALU.max))
                link(dve.reciprocal(cc, cc))
                link(dve.tensor_tensor(out=cc, in0=cc, in1=nsag[:, 24 * t:24 * t + 8], op=ALU.mult))
            for t in range(2):
                dve.wait_ge(ptc_mm, 2)
                dve.tensor_copy(PTc[:, t * P:(t + 1) * P], banks[3][:, t * P:(t + 1) * P]).then_inc(ptc_cp, 1)
            for t in range(2):
                dve.wait_ge(oc_mm, t + 1)
                heads_scaled(o_nsa[t], banks[4 + t][:, :], coef[:, 8 * t:8 * t + 1]).then_inc(oc_done, 1)
            dve.wait_ge(oc_done, 2)

            def combine(gi):
                kind, t, _ = UNITS[4 * gi]
                dve.wait_ge(pv_mm, 4 * gi + 4)
                cc = coef[:, 48:56]
                link(dve.reciprocal(cc, sums[:, 8 * gi:8 * gi + 8]))
                if kind == "mla":
                    heads_scaled(o_tmp if t == 0 else o_mla1[:, :], banks[4 + gi % 2][:, :], coef[:, 48:49]).then_inc(o_done, 1)
                    return
                which = 1 if kind == "sel" else 2
                link(dve.tensor_tensor(out=cc, in0=cc, in1=nsag[:, 24 * t + 8 * which:24 * t + 8 * which + 8], op=ALU.mult))
                link(heads_scaled(o_tmp, banks[4 + gi % 2][:, :], coef[:, 48:49]))
                dve.tensor_tensor(out=o_nsa[t], in0=o_nsa[t], in1=o_tmp, op=ALU.add).then_inc(o_done, 1)
                dve.wait_ge(o_done, gi + 1)

            N = len(UNITS)
            for n in range(N + 3):
                if 2 <= n < N + 2:
                    m = n - 2
                    w = 2 * (UNITS[m][1] + 1) * P
                    dve.wait_ge(pt_mm, m + 1)
                    if m >= 2:
                        dve.wait_ge(pv_mm, m - 1)
                    dve.tensor_copy(PT_sb[m % 2][:, 0:w], banks[2 + m % 2][:, 0:w]).then_inc(pt_cp, 1)
                if n < N:
                    kind, t, j = UNITS[n]
                    K = (t + 1) * P
                    dve.wait_ge(s_mm, n + 1)
                    if n >= 2:
                        dve.wait_ge(p_ready, 2 * (n - 1))
                    for e, h in enumerate(heads(kind, j)):
                        bias = maskM[:, t * P:t * P + K] if kind == "mla" else biasN[:, h, t * P:t * P + K]
                        m = 4 * (n % 2) + e
                        dve.tensor_tensor_reduce(out=S_sb[n % 2][:, e, 0:K], in0=banks[n % 2][:, e * K:(e + 1) * K], in1=bias,
                                                 scale=1.0, scalar=LOWEST, op0=ALU.add, op1=ALU.max, accum_out=mxs[:, m:m + 1]).then_inc(own_dve, 1)
                        own.n += 1
                    dve.wait_ge(own_dve, own.n)
                    m = 4 * (n % 2)
                    dve.tensor_scalar(out=mxs[:, m + 2:m + 4], in0=mxs[:, m:m + 2], scalar1=-1.0, scalar2=None, op0=ALU.mult).then_inc(s_max, 1)
                if n >= 6 and (n - 6) % 4 == 0:
                    combine((n - 6) // 4)
            dve.wait_ge(a_cp, 22)
            for t in range(2):
                link(dve.tensor_scalar(out=gt[:, t, :], in0=gt[:, t, :], scalar1=0.5, scalar2=0.5, op0=ALU.mult, op1=ALU.add))
            def branches(t, part_of):
                for n in (range(4), (0, 1), (2, 3))[part_of + t if t else 0]:
                    dve.wait_ge(y_mm, 4 * t + n + 1)
                    part = gt[:, t, n * 512:(n + 1) * 512]
                    dve.tensor_tensor(out=part, in0=part, in1=banks[y_bank(t, n)][:, :], op=ALU.mult).then_inc(y_used, 1)
                if part_of == 0 and t:
                    return
                dve.wait_ge(y_used, 4 * t + 4)
                dve.tensor_tensor(out=gt[:, t, 0:DM], in0=gt[:, t, 0:DM], in1=gt[:, t, DM:2 * DM], op=ALU.add).then_inc(merged, 1)

            def residual(t):
                for half in range(2):
                    dve.wait_ge(wo_mm, 2 * t + half + 1)
                    part = xs[:, t, half * 512:(half + 1) * 512]
                    dve.tensor_tensor(out=part, in0=part, in1=banks[wo_bank(t, half)][:, :], op=ALU.add).then_inc(own_dve, 1)
                own.n += 2
                dve.wait_ge(own_dve, own.n)
                dve.engine_nop().then_inc(h_ready, 1)

            def norm2(t):
                dve.wait_ge(rstd2, t + 1)
                dve.scalar_tensor_tensor(out=gt[:, t, DM:2 * DM], in0=xs[:, t, :], scalar=stat[:, 18 + t:19 + t], in1=g2b[:, :],
                                         op0=ALU.mult, op1=ALU.mult).then_inc(xt2_ready, 1)

            branches(0, 0)
            branches(1, 0)
            dve.wait_ge(g2_in, 16)
            residual(0)
            norm2(0)
            branches(1, 1)

            def top16(values, index, src, scratch):
                def then(ins):
                    link(ins)
                    dve.sem_inc(pass_dve, 1)
                then(dve.max(values[:, 0:8], src))
                then(dve.match_replace(scratch, values[:, 0:8], src, LOWEST))
                dve.max_index(index[:, 0:8], values[:, 0:8], src)
                then(dve.max(values[:, 8:16], scratch))
                then(dve.max_index(index[:, 8:16], values[:, 8:16], scratch))

            def choose(t, p):
                dve.wait_ge(key_mm, p + 1)
                dve.sem_inc(pass_dve, 1)
                for half in range(2):
                    top16(top_v[:, half, :], top_i[:, half * TOP:(half + 1) * TOP],
                          banks[6][:, t * 256 + half * NK:t * 256 + (half + 1) * NK], scrap[:, 0:NK])
                dve.tensor_copy(top_if.rearrange("p a b -> p (a b)"), top_i[:, :]).then_inc(keys_read, 1)
                link(dve.tensor_tensor(out=cand.rearrange("p (a b) -> p a b", a=TOP), in0=bc(top_v[:, 0, 0:1], [[1, TOP], [0, TOP]]),
                                       in1=bc(top_v[:, 1, 0:1], [[0, TOP], [1, TOP]]), op=ALU.add))
                dve.sem_inc(pass_dve, 1)
                top16(ts_v, pos_i, cand, scrap2)
                dve.tensor_scalar(out=d_stat[:, 0:1], in0=ts_v[:, 0:1], scalar1=-1.0, scalar2=None, op0=ALU.mult).then_inc(top_ready, 1)
                dve.tensor_scalar(out=ab_i[:, 0:TOP], in0=pos_i[:, :], scalar1=4, scalar2=None, op0=ALU.logical_shift_right)
                link(dve.tensor_scalar(out=ab_i[:, TOP:2 * TOP], in0=pos_i[:, :], scalar1=15, scalar2=None, op0=ALU.bitwise_and))
                link(dve.tensor_copy(ab_f.rearrange("p a b -> p (a b)"), ab_i[:, :]))
                for half in range(2):
                    h = (hot, hot2)[half].rearrange("p (a b) -> p a b", a=TOP)
                    link(dve.tensor_tensor(out=h, in0=bc(ab_f[:, half, 0:1], [[1, TOP], [0, TOP]]),
                                           in1=bc(io16[:, 0:1], [[0, TOP], [1, TOP]]), op=ALU.is_equal))
                    link(dve.tensor_tensor(out=h, in0=h, in1=bc(top_if[:, half, 0:1], [[0, TOP], [1, TOP]]), op=ALU.mult))
                    link(dve.tensor_reduce(out=r12[:, half, :], in_=h, axis=AXX, op=ALU.add))

            def give(t, p, first=False):
                if not first:
                    dve.wait_ge(chosen_taken, p - 1)
                dve.scalar_tensor_tensor(out=chosen[t][:, :], in0=r12[:, 0, :], scalar=float(NK), in1=r12[:, 1, :],
                                         op0=ALU.mult, op1=ALU.add).then_inc(chosen_ready, 1)

            def softmax(t, p):
                dve.wait_ge(exp_ready, p + 1)
                link(dve.reciprocal(d_stat[:, 2:3], d_stat[:, 1:2]))
                link(dve.tensor_scalar(out=soft[t], in0=soft[t], scalar1=d_stat[:, 2:3], scalar2=0.5, op0=ALU.mult, op1=ALU.mult))

            def dot(t, k, s):
                dve.wait_ge(dn_in[k % RING], (2 * s + k // RING + 1) * 16)
                row = ring_dn[:, k % RING, :]
                dve.tensor_tensor_reduce(out=row, in0=row, in1=gt[:, t, DM:2 * DM], scale=1.0, scalar=0.0,
                                         op0=ALU.mult, op1=ALU.add, accum_out=hdn[:, k:k + 1]).then_inc(dn_used, 1)

            def coefficients(t, s, first=False):
                dve.wait_ge(dn_used, (s + 1) * SLOTS)
                link(dve.tensor_tensor(out=gel[:, 0, :], in0=hdn, in1=hdn, op=ALU.mult))
                link(dve.tensor_scalar(out=gel[:, 0, :], in0=gel[:, 0, :], scalar1=GELU_C, scalar2=1.0, op0=ALU.mult, op1=ALU.add))
                dve.tensor_tensor(out=gel[:, 0, :], in0=gel[:, 0, :], in1=hdn, op=ALU.mult).then_inc(poly_ready, 1)
                dve.wait_ge(tanh_ready, s + 1)
                link(dve.scalar_tensor_tensor(out=gel[:, 2, :], in0=gel[:, 1, :], scalar=1.0, in1=hdn, op0=ALU.add, op1=ALU.mult))
                if not first:
                    dve.wait_ge(diag_ready, (s - 1) * SLOTS)
                dve.tensor_tensor(out=cof[t], in0=gel[:, 2, :], in1=soft[t], op=ALU.mult).then_inc(cof_ready, 1)

            def half_step(t_dot, s, prepare, first=False):
                for k in range(SLOTS):
                    dot(t_dot, k, s)
                    if k == RING - 1 and prepare:
                        choose(1 - t_dot, s + 1)
                        give(1 - t_dot, s + 1, first and t_dot == 0)
                coefficients(t_dot, s, first)
                if prepare:
                    softmax(1 - t_dot, s + 1)

            choose(0, 0)
            give(0, 0, first=True)
            softmax(0, 0)
            residual(1)
            norm2(1)
            dve.memset(diag[:, :, :], 0.0).then_inc(y_zero, 1)
            half_step(0, 0, True, first=True)
            half_step(1, 1, True, first=True)
            half_step(0, 2, True)
            n0 = own.n
            per = None
            with dve.Fori(1, LOOPS) as i:
                own.turn = (i - 1) * DVE_LINKS
                half_step(1, 2 * i + 1, True)
                half_step(0, 2 * i + 2, True)
            per = own.n - n0
            assert per == DVE_LINKS, per
            own.turn, own.n = 0, n0 + DVE_LINKS * (LOOPS - 1)
            half_step(1, 2 * LOOPS + 1, False)
            dve.wait_ge(gf_in, 16)
            for t in range(2):
                dve.wait_ge(y_done, t + 1)
                for half in range(2):
                    part = xs[:, t, half * 512:(half + 1) * 512]
                    dve.tensor_tensor(out=part, in0=part, in1=banks[2 * t + half][:, :], op=ALU.add).then_inc(own_dve, 1)
                own.n += 2
                dve.wait_ge(own_dve, own.n)
                dve.engine_nop().then_inc(hy_ready, 1)
            for t in range(2):
                dve.wait_ge(rstd3, t + 1)
                dve.scalar_tensor_tensor(out=xs[:, t, :], in0=xs[:, t, :], scalar=stat[:, 26 + t:27 + t], in1=gfb,
                                         op0=ALU.mult, op1=ALU.mult).then_inc(out_ready, 1)

        @block.tensor
        def _(pe):
            idn = ident[:, :]

            def mm(out_, lhsT, rhs, start=True, stop=True):
                return pe.matmul(out_, lhsT, rhs, start=start, stop=stop)

            own = Steps(pe, own_pe)

            def tr(out_, in_):
                return pe.transpose(out_, in_, idn)

            pe.wait_ge(id_ready, 1)
            for n in range(4):
                t, half = n // 2, n % 2
                pe.wait_ge(xn_ready, t + 1)
                if n >= 2:
                    pe.wait_ge(xt_cp, n - 1)
                for k in range(4):
                    last = tr(banks[2 + n % 2][:, k * P:(k + 1) * P], gt[:, t, (4 * half + k) * P:(4 * half + k + 1) * P])
                last.then_inc(xt_mm, 1)
            pe.wait_ge(xt_cp, 4)

            unit = [0]

            def a_bank():
                u = unit[0]
                if u >= 2:
                    pe.wait_ge(a_cp, u - 1)
                unit[0] += 1
                return banks[6 + u % 2]

            def transposed(w, rows):
                b = a_bank()
                for k in range(KC):
                    last = mm(b[:, 0:TOK], rows(w[:, k, :]), xTv[:, k, :], k == 0, k == KC - 1)
                return last.then_inc(a_mm, 1)

            def by_token(w, t, c0, n):
                b = a_bank()
                for k in range(KC):
                    last = mm(b[:, 0:n], xTv[:, k, tok_rows[t]], w[:, k, c0:c0 + n], k == 0, k == KC - 1)
                return last.then_inc(a_mm, 1)

            def arrived(c):
                pe.wait_ge(win_in[c % 2], 16 * (c // 2 + (0 if c % 2 and c > 3 else 1)))

            gate_done = [0]

            def gate_step(upto):
                while gate_done[0] < upto:
                    m = gate_done[0]
                    v, k = m // KC, m % KC
                    c, t = v // 2, v % 2
                    if k == 0:
                        if t == 0:
                            arrived(4 + c)
                        a_bank()
                    last = mm(banks[6 + v % 2][:, :], xTv[:, k, tok_rows[t]], chunk(4 + c)[:, k, :], k == 0, k == KC - 1)
                    if k == KC - 1:
                        last.then_inc(a_mm, 1)
                        if t == 1:
                            pe.wait_ge(a_mm, unit[0])
                            pe.sem_inc(win_used, 1)
                    gate_done[0] += 1

            arrived(0)
            by_token(chunk(0), 0, 0, MLA_W)
            by_token(chunk(0), 1, 0, MLA_W)
            pe.wait_ge(a_mm, 2)
            pe.sem_inc(win_used, 1)
            arrived(1)
            for b in range(3):
                transposed(chunk(1), lambda w, b=b: w[:, b * P:(b + 1) * P])
            for t in range(2):
                by_token(chunk(1), t, 384, P)
            pe.wait_ge(a_mm, 7)
            pe.sem_inc(win_used, 1)
            for t in range(2):
                pe.wait_ge(mla_scaled, 2 * t + 2)
                for b in range(3):
                    last = tr(banks[2 + t][:, b * P:(b + 1) * P], mla_tok[:, t, b * P:(b + 1) * P])
                last.then_inc(mt_mm, 1)
            arrived(2)
            transposed(chunk(2), lambda w: w[:, 0:P])
            for t in range(2):
                by_token(chunk(2), t, P, P + 24)
            pe.wait_ge(a_mm, 10)
            pe.sem_inc(win_used, 1)
            pe.wait_ge(sk_sem, 32)
            for n in range(2):
                last = tr(banks[0][:, n * P:(n + 1) * P], sk_in[:, n * P:(n + 1) * P])
            last.then_inc(sk_mm, 1)
            pe.wait_ge(mla_w_in, 96)
            pe.wait_ge(mt_cp, 2)
            pe.wait_ge(sk_cp, 1)
            for b in range(2):
                for e in range(2):
                    pr = 2 * b + e
                    for k in range(2):
                        last = mm(banks[b][:, e * 256:(e + 1) * 256], w_uqn[:, k, pr * P:(pr + 1) * P], mlaT[:, k, :], k == 0, k == 1)
                last.then_inc(j_mm, 1)
            for t in range(2):
                for k in range(2):
                    last = mm(banks[4][:, t * 256:(t + 1) * 256], mlaT[:, k, tok_rows[t]], w_uqp[:, k, :], k == 0, k == 1)
            last.then_inc(j_mm, 1)
            for n, b in enumerate((5, 2)):
                for e in range(2):
                    pr = 2 * n + e
                    last = mm(banks[b][:, e * 256:(e + 1) * 256], w_uk[:, pr * P:(pr + 1) * P], mlaT[:, 2, :])
                last.then_inc(j_mm, 1)
            for t, b in enumerate((3, 0)):
                if t == 1:
                    pe.wait_ge(j_act, 1)
                mm(banks[b][:, :], mlaT[:, 2, tok_rows[t]], w_uv).then_inc(j_mm, 1)
            pe.wait_ge(win_q_in, 16 * 2 * KC)
            for j in range(4):
                transposed(chunk(3), lambda w, j=j: w[:, j * P:(j + 1) * P])
            pe.wait_ge(a_mm, 14)
            pe.sem_inc(win_used, 1)
            for t, b in enumerate((1, 4)):
                pe.wait_ge(roped, 2 if t else 1)
                if t == 0:
                    pe.wait_ge(j_act, 2)
                for c in range(3):
                    last = tr(banks[b][:, c * P:(c + 1) * P], rope[:, t, 4 * c:4 * c + 4, :].rearrange("p a b -> p (a b)"))
                last.then_inc(pe_mm, 1)
            pe.wait_ge(blk_ready, 4)
            pe.wait_ge(cmp_w_in, 80)
            pe.wait_ge(j_act, 3)
            for v in range(2):
                for l in range(16):
                    last = mm(banks[5][:, 32 * v:32 * v + 32], w1[v][:, l, :], blk[v][:, l, :], l == 0, l == 15)
            last.then_inc(hid_mm, 1)
            gate_step(GATE_HID)
            pe.wait_ge(hid_ready, 1)
            pe.wait_ge(j_act, 4)
            mm(banks[2][:, 0:32], w2kd, cmpw[:, 4, 0:32]).then_inc(kc_mm, 1)
            mm(banks[2][:, 64:128], hvrep, w2v).then_inc(kc_mm, 1)
            pe.wait_ge(kc_cp, 1)
            pe.wait_ge(j_dve, 2)
            for t in range(2):
                if t == 1:
                    pe.wait_ge(pe_cp, 1)
                for h in range(NH):
                    g, j = h // 4, h % 4
                    rows = slice(g * HD, (g + 1) * HD)
                    last = mm(banks[t][:, h * 16:(h + 1) * 16], qT[rows, j, tok_rows[t]], kcT[rows, 16 * g:16 * g + 16])
                    if h == 3:
                        own.link(last)
                last.then_inc(sc_mm, 1)
            gate_step(GATE_CMP)
            for t in range(2):
                pe.wait_ge(pc_ready, t + 1)
                tr(banks[3][:, t * P:(t + 1) * P], Sc[:, t * P:(t + 1) * P]).then_inc(ptc_mm, 1)
            gate_step(GATE_PRE)
            pe.wait_ge(vbd_ready, 1)
            pe.wait_ge(pe_cp, 2)
            for t in range(2):
                pe.wait_ge(ptc_cp, t + 1)
                mm(banks[4 + t][:, :], PTc[:, t * P:(t + 1) * P], VBD).then_inc(oc_mm, 1)

            def scores(n):
                kind, t, j = UNITS[n]
                K = (t + 1) * P
                if n < 2:
                    pe.wait_ge(sc_max, 2)
                else:
                    pe.wait_ge(s_max, n - 1)
                for e, h in enumerate(heads(kind, j)):
                    dst = banks[n % 2][:, e * K:(e + 1) * K]
                    rows = slice(e * HD, (e + 1) * HD)
                    if e:
                        yield own.mark(last)
                        own.wait()
                    if kind == "mla":
                        quad = slice(32 * (h % 4), 32 * (h % 4) + 32)
                        yield own.mark(mm(dst, qnT[rows, j, tok_rows[t]], knT[rows, j, 0:K], True, False))
                        own.wait()
                        last = pe.matmul(dst, peT[quad, h // 4, tok_rows[t]], peT[quad, 2, 0:K], start=False, stop=True,
                                         tile_position=(32 * (h % 4), 0))
                    else:
                        last = mm(dst, qT[rows, j, tok_rows[t]], keyT[0 if kind == "sel" else 1][rows, 0:K])
                last.then_inc(s_mm, 1)

            def turn(n):
                t = UNITS[n][1]
                pe.wait_ge(p_ready, 2 * n + 2)
                if n >= 2:
                    pe.wait_ge(pt_cp, n - 1)
                elif n == 1:
                    pe.wait_ge(ptc_cp, 2)
                for e in range(2):
                    for c in range(t + 1):
                        at_ = (e * (t + 1) + c) * P
                        last = tr(banks[2 + n % 2][:, at_:at_ + P], P_sb[n % 2][:, e, c * P:(c + 1) * P])
                last.then_inc(pt_mm, 1)

            def values(n):
                kind, t, j = UNITS[n]
                gi = n // 4
                pe.wait_ge(pt_cp, n + 1)
                if n % 4 == 0:
                    if gi < 2:
                        pe.wait_ge(oc_done, gi + 1)
                    else:
                        pe.wait_ge(o_done, gi - 1)
                for e, h in enumerate(heads(kind, j)):
                    for c in range(t + 1):
                        at_ = (e * (t + 1) + c) * P
                        if kind == "mla":
                            v = vml[:, c, h * HD:(h + 1) * HD]
                        else:
                            v = val[0 if kind == "sel" else 1][:, c, e * HD:(e + 1) * HD]
                        last = mm(banks[4 + gi % 2][:, h * HD:(h + 1) * HD], PT_sb[n % 2][:, at_:at_ + P], v, c == 0, c == t)
                last.then_inc(pv_mm, 1)

            N = len(UNITS)
            pe.wait_ge(a_cp, 14)
            pe.wait_ge(j_dve, 2)
            pe.wait_ge(mask_ready, 17)
            for n in range(N + 3):
                work = []
                if 2 <= n < N + 2:
                    work.append(lambda: turn(n - 2))
                if n >= 3:
                    work.append(lambda: values(n - 3))
                if n < N:
                    work.append(lambda: gate_step(gate_upto(n)))
                    for _ in scores(n):
                        if work:
                            work.pop(0)()
                for rest in work:
                    rest()
            for b, (src, need) in enumerate(((o_nsa[0], 3), (o_nsa[1], 4), (o_tmp, 5), (o_mla1[:, :], 6))):
                pe.wait_ge(o_done, need)
                if b == 2:
                    pe.wait_ge(pt_cp, N)
                for k in range(4):
                    last = tr(banks[b][:, k * P:(k + 1) * P], src[:, k * P:(k + 1) * P])
                last.then_inc(ot_mm, 1)
            pe.wait_ge(wbn_in, 16)
            pe.wait_ge(wbm_in, 16)
            pe.wait_ge(ot_cp, 4)
            pe.wait_ge(a_cp, 22)
            def branch(t, n):
                part, half = n // 2, n % 2
                for k in range(4):
                    last = mm(banks[y_bank(t, n)][:, :], oTv[:, 4 * part + k, tok_rows[t]],
                              (wbn, wbm)[part][:, k, half * 512:(half + 1) * 512], k == 0, k == 3)
                last.then_inc(y_mm, 1)

            def mergedT(t):
                pe.wait_ge(merged, t + 1)
                for half in range(2):
                    for k in range(4):
                        last = tr(banks[mg_bank(t, half)][:, k * P:(k + 1) * P], gt[:, t, (4 * half + k) * P:(4 * half + k + 1) * P])
                    last.then_inc(mg_mm, 1)

            def w_out(t):
                pe.wait_ge(mg_cp, 2 * t + 2)
                for half in range(2):
                    for k in range(KC):
                        last = mm(banks[wo_bank(t, half)][:, :], xTv[:, k, tok_rows[t]], wo[:, k, half * 512:(half + 1) * 512], k == 0, k == KC - 1)
                    last.then_inc(wo_mm, 1)

            def normedT(t):
                pe.wait_ge(xt2_ready, t + 1)
                for half in range(2):
                    for k in range(4):
                        last = tr(banks[xt2_bank(t, half)][:, k * P:(k + 1) * P],
                                  gt[:, t, DM + (4 * half + k) * P:DM + (4 * half + k + 1) * P])
                    last.then_inc(xt2_mm, 1)


            def query(t, head, p, first=False):
                if not first:
                    pe.wait_ge(q_cp, p)
                for k in range(KC):
                    rhs = wq[:, k, bass.ds(head * 256, 256)]
                    last = mm(banks[4][:, t * 256:(t + 1) * 256], oTv[:, k, tok_rows[t]], rhs, k == 0, k == KC - 1)
                last.then_inc(q_mm, 1)

            def queryT(t, p, first=False):
                pe.wait_ge(q_cp, p + 1)
                if not first:
                    pe.wait_ge(qt_cp, p)
                for half in range(2):
                    last = tr(banks[5][:, t * 256 + half * P:t * 256 + (half + 1) * P], q_tok[t][:, half * P:(half + 1) * P])
                last.then_inc(qt_mm, 1)

            def key_scores(t, p, first=False):
                pe.wait_ge(qt_cp, p + 1)
                if not first:
                    pe.wait_ge(keys_read, p)
                for half in range(2):
                    last = mm(banks[6][:, t * 256 + half * P:t * 256 + (half + 1) * P], q_T[t][:, half * P:(half + 1) * P],
                              skT[:, half * P:(half + 1) * P])
                last.then_inc(key_mm, 1)

            def weigh(t, k, s, stop=False):
                pe.wait_ge(diag_ready, s * SLOTS + k + 1)
                pe.wait_ge(up_in[k % RING], (2 * s + k // RING + 1) * 16)
                for half in range(2):
                    last = mm(banks[2 * t + half][:, :], diag[:, k % RING, :], ring_up[:, k % RING, half * 512:(half + 1) * 512],
                              False, stop)
                last.then_inc(up_used, 1)

            def half_step(t, s, head, prepare, stop=False):
                if prepare:
                    query(t, head, s + 2)
                for k in range(SLOTS):
                    if k == 4 and prepare:
                        queryT(t, s + 2)
                    if k == 8 and prepare:
                        key_scores(t, s + 2)
                    weigh(t, k, s, stop and k == SLOTS - 1)

            for n in range(4):
                branch(0, n)
            for n in range(2):
                branch(1, n)
            mergedT(0)
            pe.wait_ge(wo_in, 16)
            w_out(0)
            pe.wait_ge(y_used, 4)
            for n in range(2, 4):
                branch(1, n)
            normedT(0)
            pe.wait_ge(xt2_cp, 2)
            pe.wait_ge(wq_in, 16)
            query(0, 0, 0, first=True)
            mergedT(1)
            queryT(0, 0, first=True)
            key_scores(0, 0, first=True)
            pe.wait_ge(y_used, 8)
            w_out(1)
            normedT(1)
            pe.wait_ge(xt2_cp, 4)
            query(1, 0, 1)
            queryT(1, 1)
            key_scores(1, 1)
            pe.wait_ge(h_ready, 2)
            pe.wait_ge(y_zero, 1)
            for b in range(4):
                last = mm(banks[b][:, :], diag[:, 0, :], diag[:, 0:4, :], True, False)
            last.then_inc(y_started, 1)
            half_step(0, 0, 1, True)
            half_step(1, 1, 1, True)
            with pe.Fori(1, LOOPS) as i:
                half_step(0, 2 * i, i + 1, True)
                half_step(1, 2 * i + 1, i + 1, True)
            half_step(0, 2 * LOOPS, 0, False, stop=True)
            pe.wait_ge(up_used, (2 * LOOPS + 1) * SLOTS)
            pe.sem_inc(y_done, 1)
            half_step(1, 2 * LOOPS + 1, 0, False, stop=True)
            pe.wait_ge(up_used, (2 * LOOPS + 2) * SLOTS)
            pe.sem_inc(y_done, 1)


_NAMES = {"w_in": "w_in", "norm1_g": "norm1_g", "pos_k": "nsa_cmp_pos_k", "w1k": "nsa_cmp_w1_k", "w2k": "nsa_cmp_w2_k",
          "pos_v": "nsa_cmp_pos_v", "w1v": "nsa_cmp_w1_v", "w2v": "nsa_cmp_w2_v", "mla_q_norm_g": "mla_q_norm_g",
          "mla_kv_norm_g": "mla_kv_norm_g", "w_uq": "mla_w_uq", "w_ukv": "mla_w_ukv", "wb_nsa": "w_branch_nsa",
          "wb_mla": "w_branch_mla", "w_out": "w_out", "norm2_g": "norm2_g", "w_query": "peer_w_query",
          "sub_keys_1": "peer_sub_keys_1", "sub_keys_2": "peer_sub_keys_2", "expert_down": "peer_expert_down",
          "expert_up": "peer_expert_up", "norm_f_g": "norm_f_g", "x": "x", "positions": "positions"}


def kernel(**inputs):
    import concourse.bacc as bacc
    from concourse.bass_utils import run_bass_kernel_spmd as run

    nc = bacc.Bacc("TRN2", target_bir_lowering=False, num_devices=1)
    arrays, args = {}, {}
    for short, name in _NAMES.items():
        v = np.ascontiguousarray(inputs[name])
        if v.ndim == 3:
            v = v[0]
        arrays[f"in_{short}"] = v
        args[short] = nc.dram_tensor(f"in_{short}", v.shape, mybir.dt.from_np(v.dtype), kind="ExternalInput").ap()
    out = nc.dram_tensor("out", (TOK, DM), F32, kind="ExternalOutput").ap()
    block_program(nc, args, out)
    r = run(nc, [arrays], core_ids=[0])
    return r.results[0]["out"].reshape(1, TOK, DM)
```

```python
from contextlib import ExitStack

import numpy as np

import concourse.bass as bass
from concourse import mybir

F32 = mybir.dt.float32
U32 = mybir.dt.uint32
I32 = mybir.dt.int32
ALU = mybir.AluOpType
ACT = mybir.ActivationFunctionType
AXX = mybir.AxisListType.X

P = 128
DM = 1024
TOK = 256
NT = TOK // P
KC = DM // P
HD = 64
NH = 8
NCMP = TOK // 16
ROPE = 32
QKW = HD + ROPE
NK = 128
TOP = 16
EPS = 1e-6
NEG = -1e30
LOWEST = -3e38
GELU_C = 0.044715
GELU_S = float(np.sqrt(2.0 / np.pi))
RING = 8
SLOTS = TOP
DVE_LINKS = 46
LOOPS = NH - 1
LAST = 2 * LOOPS + 1
ADDED = (9, 11, 14, 15)
WEIGHED = [k for k in range(SLOTS) if k not in ADDED]

C_KCMP, C_VCMP, C_KSEL, C_VSEL, C_KWIN, C_VWIN, C_GATE, C_CQ, C_GN = (
    512, 640, 768, 896, 1024, 1152, 1280, 1304, 1720)
MLA_W = 416
CHUNKS = [(C_CQ, MLA_W), (C_KCMP, 512), (C_KWIN, 280), (0, 512)] + [(C_GN + 512 * c, 512) for c in range(4)]
CHUNK_UNITS = (2, 7, 10, 14, 16, 18, 20, 22)


class Steps:

    def __init__(self, eng, sem):
        self.eng, self.sem, self.n, self.turn = eng, sem, 0, 0

    def link(self, ins):
        ins.then_inc(self.sem, 1)
        self.n += 1
        self.eng.wait_ge(self.sem, self.turn + self.n)

    def mark(self, ins):
        ins.then_inc(self.sem, 1)
        self.n += 1

    def wait(self):
        self.eng.wait_ge(self.sem, self.turn + self.n)


def bc(ap, dims):
    return bass.AP(ap.tensor, ap.offset, [list(ap.ap[0])] + [list(d) for d in dims])


def block_program(nc, a, out):
    ctx = ExitStack()
    with ctx:
        def sb(name, words, dt=F32):
            return ctx.enter_context(nc.sbuf_tensor(name, [P, words], dt))

        def sem(name):
            return ctx.enter_context(nc.semaphore(name))

        region_q = sb("region_q", 16384)
        region_w = sb("region_w", 16384)
        x_sb = sb("x_sb", 2048)
        gates = sb("gates", 4096)
        xT = sb("xT", 2048)
        oT = sb("oT", 2048)
        g2b = sb("g2b", 1024)
        pool_bd = sb("pool_bd", 6400)
        ident = sb("ident", 128)
        skT = sb("skT", 256)
        g1c = sb("g1c", 8)
        gmc = sb("gmc", 3)
        stat = sb("stat", 64)
        io16 = sb("io16", 16)
        o_mla1 = sb("o_mla1", 512)

        banks = [ctx.enter_context(nc.psum_tensor(f"bank{i}", [P, 512], F32)) for i in range(8)]

        def view(t, at, *dims):
            n = int(np.prod(dims))
            v = t[:, at:at + n]
            if len(dims) == 2:
                return v.rearrange("p (a b) -> p a b", a=dims[0])
            if len(dims) == 3:
                return v.rearrange("p (a b c) -> p a b c", a=dims[0], b=dims[1])
            return v

        xs = view(x_sb, 0, 2, 1024)
        gt = view(gates, 0, 2, 2048)
        xTv = view(xT, 0, 8, 256)
        gfb = view(xT, 0, 1024)
        oTv = view(oT, 0, 8, 256)
        win = [view(region_q, 4096 * b, 4096) for b in range(2)]

        def chunk(c):
            return win[c % 2][:, 0:8 * CHUNKS[c][1]].rearrange("p (k n) -> p k n", k=KC)

        at = [8192]

        def in_q(*dims):
            v = view(region_q, at[0], *dims)
            at[0] += int(np.prod(dims))
            return v
        biasN = in_q(NH, 384)
        maskM = in_q(384)
        S_sb = [in_q(2, 256) for _ in range(2)]
        P_sb = [in_q(2, 256) for _ in range(2)]
        PT_sb = [in_q(512) for _ in range(2)]
        o_nsa = [in_q(512) for _ in range(2)]
        o_tmp = in_q(512)
        sk_in = o_tmp[:, 0:256]
        Sc = o_tmp[:, 256:512]
        assert at[0] <= 16384
        wq = view(region_q, 0, KC, 2048)
        wbn = view(region_w, 0, 4, 1024)
        wbm = view(region_w, 4096, 4, 1024)
        wo = view(region_w, 8192, KC, 1024)
        at[0] = 4096

        def in_w(*dims):
            v = view(region_w, at[0], *dims)
            at[0] += int(np.prod(dims))
            return v
        w_uqn, w_uqp = in_w(2, 512), in_w(2, 256)
        mlaT = in_w(3, 256)
        rope = in_w(2, 12, 32)
        w_uk, w_uv = in_w(512), in_w(512)
        w1 = [in_w(16, P) for _ in range(2)]
        kvc = [in_w(256) for _ in range(2)]
        kk = [[in_w(256) for _ in range(2)] for _ in range(2)]
        blk = [in_w(16, 32) for _ in range(2)]
        mla_tok = in_w(2, MLA_W)
        ropt = [in_w(12, 16) for _ in range(2)]
        trig = in_w(2, 2, 16)
        ang = in_w(5, 32)
        pos_row = in_w(2, 16)
        w2kd, w2v, hvrep = sb("w2kd", P)[:, :], sb("w2v", HD)[:, :], sb("hvrep", P)[:, :]
        cmpw = view(sb("cmpw", 320), 0, 5, 64)
        assert at[0] <= 16384
        ring_dn = view(region_w, 0, RING, 1024)
        ring_up = view(region_w, 8192, RING, 1024)
        at[0] = 0

        def in_b(*dims):
            v = view(pool_bd, at[0], *dims)
            at[0] += int(np.prod(dims))
            return v
        qT = in_b(4, 256)
        keyT = [in_b(256) for _ in range(2)]
        val = [in_b(2, P) for _ in range(2)]
        qnT = in_b(4, 256)
        knT = in_b(4, 256)
        vml = in_b(2, 512)
        peT = in_b(3, 256)
        VBD = in_b(512)
        nsag = sb("nsag", 48)
        kcT = sb("kcT", 32)
        biasC = sb("biasC", 256)
        maskC = sb("maskC", 32)
        blkmask = sb("blkmask", 8)
        PTc = sb("PTc", 256)
        coef = sb("coef", 64)
        sums = sb("sums", 56)
        mxs = sb("mxs", 8)
        assert at[0] <= 6400, at[0]
        at[0] = 0
        q_tok = [in_b(256) for _ in range(2)]
        q_T = [in_b(256) for _ in range(2)]
        top_v = in_b(2, TOP)
        top_if = in_b(2, TOP)
        scrap = in_b(256)
        cand = in_b(256)
        scrap2 = in_b(256)
        hot = in_b(512)
        ts_v = in_b(TOP)
        ab_f = in_b(2, TOP)
        r12 = in_b(2, TOP)
        soft = [in_b(TOP) for _ in range(2)]
        hdn = in_b(TOP)
        gel = in_b(3, TOP)
        cof = [in_b(TOP) for _ in range(2)]
        diag = in_b(RING, P)
        d_stat = in_b(16)
        assert at[0] <= 6400
        top_i = sb("top_i", 32, U32)
        pos_i = sb("pos_i", 16, U32)
        ab_i = sb("ab_i", 32, U32)
        chosen = [sb(f"chosen{t}", TOP, U32) for t in range(2)]
        idx_dn = [sb(f"idx_dn{t}", TOP, U32) for t in range(2)]
        idx_up = [sb(f"idx_up{t}", TOP, U32) for t in range(2)]
        pos_i32 = sb("pos_i32", 2, I32)

        x_in = [sem(f"x_in{t}") for t in range(2)]
        win_in = [sem(f"win_in{b}") for b in range(2)]
        win_q_in = sem("win_q_in")
        g1_in = sem("g1_in")
        vec_in, mla_w_in, cmp_w_in, g2_in, sk_sem, pos_in = (sem(n) for n in (
            "vec_in", "mla_w_in", "cmp_w_in", "g2_in", "sk_sem", "pos_in"))
        wbn_in, wbm_in, wo_in, wq_in, gf_in = (sem(n) for n in ("wbn_in", "wbm_in", "wo_in", "wq_in", "gf_in"))
        kk_in = sem("kk_in")
        id_ready, mask_ready, const_ready = sem("id_ready"), sem("mask_ready"), sem("const_ready")
        sk_mm, sk_cp = sem("sk_mm"), sem("sk_cp")
        rstd1, rstd_mla, rstd2, rstd3 = (sem(n) for n in ("rstd1", "rstd_mla", "rstd2", "rstd3"))
        ssq = [sem(f"ssq_x{t}") for t in range(2)]
        xn_ready = sem("xn_ready")
        xt_mm, xt_cp = sem("xt_mm"), sem("xt_cp")
        a_mm, a_cp = sem("a_mm"), sem("a_cp")
        ssq_mla, mla_scaled = sem("ssq_mla"), sem("mla_scaled")
        mt_mm, mt_cp = sem("mt_mm"), sem("mt_cp")
        j_mm = sem("j_mm")
        j_act, j_dve = sem("j_act"), sem("j_dve")
        ang_ready, trig_ready = sem("ang_ready"), sem("trig_ready")
        roped = sem("roped")
        pe_mm, pe_cp = sem("pe_mm"), sem("pe_cp")
        blk_ready = sem("blk_ready")
        hid_mm, hid_u, hid_t, hid_ready = sem("hid_mm"), sem("hid_u"), sem("hid_t"), sem("hid_ready")
        kc_mm, kc_cp, vbd_ready = sem("kc_mm"), sem("kc_cp"), sem("vbd_ready")
        sc_mm, sc_max, sc_exp, pc_ready = sem("sc_mm"), sem("sc_max"), sem("sc_exp"), sem("pc_ready")
        ptc_mm, ptc_cp, oc_mm, oc_done = sem("ptc_mm"), sem("ptc_cp"), sem("oc_mm"), sem("oc_done")
        s_mm, s_max, p_ready = sem("s_mm"), sem("s_max"), sem("p_ready")
        pt_mm, pt_cp, pv_mm, o_done = sem("pt_mm"), sem("pt_cp"), sem("pv_mm"), sem("o_done")
        ot_mm, ot_cp = sem("ot_mm"), sem("ot_cp")
        y_mm, y_used, merged = sem("y_mm"), sem("y_used"), sem("merged")
        mg_mm, mg_cp, wo_mm, h_ready = sem("mg_mm"), sem("mg_cp"), sem("wo_mm"), sem("h_ready")
        ssq2, xt2_ready, xt2_mm, xt2_cp = sem("ssq2"), sem("xt2_ready"), sem("xt2_mm"), sem("xt2_cp")
        q_mm, q_cp, qt_mm, qt_cp, key_mm = (sem(n) for n in ("q_mm", "q_cp", "qt_mm", "qt_cp", "key_mm"))
        keys_read, top_ready, exp_ready, soft_ready = (sem(n) for n in ("keys_read", "top_ready", "exp_ready", "soft_ready"))
        chosen_ready, chosen_taken = sem("chosen_ready"), sem("chosen_taken")
        dn_in = [sem(f"dn_in{r}") for r in range(RING)]
        up_in = [sem(f"up_in{r}") for r in range(RING)]
        dn_used, up_used = sem("dn_used"), sem("up_used")
        poly_ready, tanh_ready, cof_ready, diag_ready = (sem(n) for n in ("poly_ready", "tanh_ready", "cof_ready", "diag_ready"))
        y_zero, y_started, y_done = sem("y_zero"), sem("y_started"), sem("y_done")
        hy_ready, ssq3, out_ready, out_sem = sem("hy_ready"), sem("ssq3"), sem("out_ready"), sem("out_sem")
        pass_pool = sem("pass_pool")
        pass_dve = sem("pass_dve")
        own_pe = sem("own_pe")
        own_dve, own_act, own_pool = sem("own_dve"), sem("own_act"), sem("own_pool")

        UNITS = [(kind, t, j) for kind in ("sel", "win", "mla") for t in range(2) for j in range(4)]

        def heads(kind, j):
            return (2 * j, 2 * j + 1) if kind == "mla" else (j, 4 + j)

        GATE_MM = 4 * NT * KC

        GATE_HID, GATE_CMP, GATE_PRE = 11, 18, 20

        def gate_upto(n):
            return min(GATE_MM, GATE_PRE + (GATE_MM - GATE_PRE) * (n + 1) // (len(UNITS) + 1))

        def gate_tanh(act, v):
            c, t = v // 2, v % 2
            act.wait_ge(a_mm, 14 + v + 1)
            act.activation(gt[:, t, 512 * c:512 * (c + 1)], banks[6 + v % 2][:, :], ACT.Tanh, scale=0.5).then_inc(a_cp, 1)

        def view_trig_in(v):
            return v[:, 3:5, :].rearrange("p c (t f) -> p c t f", t=2)

        def mg_bank(t, half):
            return ((4, 5), (7, 2))[t][half]

        def xt2_bank(t, half):
            return ((4, 5), (7, 6))[t][half]

        def wo_bank(t, half):
            return 2 * (1 - t) + half

        def y_bank(t, n):
            return ((4, 6, 7, 5), (0, 1, 7, 3))[t][n]

        w_in = a["w_in"]
        tok_rows = [slice(t * P, (t + 1) * P) for t in range(2)]

        def normed(t, half):
            return gt[:, t, DM + half * 512:DM + (half + 1) * 512]

        cols = [slice(half * 512, (half + 1) * 512) for half in range(2)]

        block = ctx.enter_context(nc.Block())

        @block.sync
        def _(sp):
            def load_chunk(c):
                c0, n = CHUNKS[c]
                if c >= 2:
                    sp.wait_ge(a_mm, CHUNK_UNITS[c - 2])
                if c != 3:
                    sp.dma_start(chunk(c), w_in[:, c0:c0 + n].rearrange("(k p) n -> p k n", p=P)).then_inc(win_in[c % 2], 16)
                    return
                pairs = chunk(c).rearrange("p k (j g c) -> p k j g c", j=4, g=2)
                for g in range(2):
                    for k in range(KC):
                        sp.dma_start(pairs[:, k, :, g, :], w_in[k * P:(k + 1) * P, 256 * g:256 * (g + 1)].rearrange(
                            "p (j c) -> p j c", j=4)).then_inc(win_q_in, 16)

            for t in range(2):
                sp.dma_start(xs[:, t, :], a["x"][tok_rows[t], :]).then_inc(x_in[t], 16)
            load_chunk(0)
            load_chunk(1)
            uq = a["w_uq"].rearrange("(k p) (h c) -> p k h c", p=P, h=NH)
            ukv = a["w_ukv"].rearrange("p (h c) -> p h c", h=NH)
            for k in range(2):
                sp.dma_start(w_uqn[:, k, :].rearrange("p (h c) -> p h c", h=NH), uq[:, k, :, 0:HD]).then_inc(mla_w_in, 16)
                sp.dma_start(w_uqp[:, k, :].rearrange("p (h c) -> p h c", h=NH), uq[:, k, :, HD:QKW]).then_inc(mla_w_in, 16)
            sp.dma_start(w_uk.rearrange("p (h c) -> p h c", h=NH), ukv[:, :, 0:HD]).then_inc(mla_w_in, 16)
            sp.dma_start(w_uv.rearrange("p (h c) -> p h c", h=NH), ukv[:, :, HD:2 * HD]).then_inc(mla_w_in, 16)
            for v, name in enumerate(("w1k", "w1v")):
                sp.dma_start(w1[v], a[name].rearrange("(l p) n -> p l n", p=P)).then_inc(cmp_w_in, 16)
            for c in range(2):
                sp.dma_start(w2kd[:, c * HD:(c + 1) * HD], a["w2k"]).then_inc(cmp_w_in, 16)
            sp.dma_start(w2v, a["w2v"]).then_inc(cmp_w_in, 16)
            load_chunk(2)
            for v in range(2):
                sp.wait_ge(a_cp, 3 + v)
                for g in range(2):
                    rows = slice(g * HD, (g + 1) * HD)
                    sp.dma_start(kk[v][g][0:HD, :], kvc[v][rows, :]).then_inc(kk_in, 16)
                    sp.dma_start(kk[v][g][HD:P, 0:TOK - 1], kvc[v][rows, 1:TOK]).then_inc(kk_in, 16)
            load_chunk(3)
            for c in range(4, 8):
                load_chunk(c)
                if c == 5:
                    sp.dma_start(wbn, a["wb_nsa"].rearrange("(k p) n -> p k n", p=P)).then_inc(wbn_in, 16)
            sp.wait_ge(pe_cp, 2)
            sp.wait_ge(vbd_ready, 1)
            sp.wait_ge(kc_cp, 1)
            sp.dma_start(wbm, a["wb_mla"].rearrange("(k p) n -> p k n", p=P)).then_inc(wbm_in, 16)
            sp.dma_start(wo, a["w_out"].rearrange("(k p) n -> p k n", p=P)).then_inc(wo_in, 16)
            sp.wait_ge(ot_cp, 4)
            sp.wait_ge(a_mm, CHUNK_UNITS[-1])
            sp.dma_start(wq, a["w_query"].rearrange("(k p) n -> p k n", p=P)).then_inc(wq_in, 16)
            sp.wait_ge(wo_mm, 4)
            sp.dma_start(gfb, a["norm_f_g"].rearrange("(o n) -> o n", o=1).broadcast_to([P, DM])).then_inc(gf_in, 16)
            sp.wait_ge(out_ready, 1)
            sp.dma_start(out[tok_rows[0], :], xs[:, 0, :]).then_inc(out_sem, 16)
            for half in range(2):
                sp.wait_ge(out_ready, half + 2)
                sp.dma_start(out[tok_rows[1], cols[half]], xs[:, 1, cols[half]]).then_inc(out_sem, 16)
            sp.wait_ge(out_sem, 48)

        @block.gpsimd
        def _(pool):
            own = Steps(pool, own_pool)
            pool.dma_start(g1c[:, :], a["norm1_g"].rearrange("o (k p) -> p (o k)", p=P), allow_slow_non_contiguous=True).then_inc(g1_in, 16)
            pool.dma_start(g2b[:, :], a["norm2_g"].broadcast_to([P, DM])).then_inc(g2_in, 16)

            own.link(pool.memset(ident[:, :], 0.0))
            pool.affine_select(out=ident[:, :], in_=ident[:, :], compare_op=ALU.not_equal, fill=1.0, base=0,
                               pattern=[[-1, P]], channel_multiplier=1).then_inc(id_ready, 1)
            def rstd(dst, src, n):
                own.link(pool.tensor_scalar(out=dst, in0=src, scalar1=1.0 / n, scalar2=EPS, op0=ALU.mult, op1=ALU.add))
                return pool.tensor_tensor(out=dst, in0=dst, in1=stat[:, 63:64], op=ALU.pow)

            own.link(pool.memset(stat[:, 63:64], -0.5))

            for t in range(2):
                pool.wait_ge(ssq[t], 1)
                rstd(stat[:, 2 + t:3 + t], stat[:, t:t + 1], DM).then_inc(rstd1, 1)
            for j in range(16):
                pool.memset(ang[:, 0, j:j + 1], float(np.float32(10000.0) ** np.float32(-2.0 * j / ROPE)))
            own.link(pool.iota(io16[:, :], [[1, 16]], base=0, channel_multiplier=0, allow_small_or_imprecise_dtypes=True))
            pool.engine_nop().then_inc(const_ready, 1)
            for v in range(2):
                pool.memset(blk[v][:, :, :], 0.0)
            own.link(pool.memset(maskM, 0.0))
            for t in range(2):
                cols = maskM[:, t * P:t * P + (t + 1) * P]
                own.link(pool.affine_select(out=cols, in_=cols, compare_op=ALU.is_ge, fill=NEG, base=t * P,
                                            pattern=[[-1, (t + 1) * P]], channel_multiplier=1))
            for t in range(2):
                n = (t + 1) * P
                own.link(pool.iota(biasN[:, 0, t * P:t * P + n], [[-1, n]], base=t * P, channel_multiplier=1,
                                   allow_small_or_imprecise_dtypes=True))
            for h in range(NH - 1, -1, -1):
                own.link(pool.tensor_scalar(out=biasN[:, h, :], in0=biasN[:, 0, :], scalar1=-(2.0 ** -(h + 1)), scalar2=None, op0=ALU.mult))
                for t in range(2):
                    cols = biasN[:, h, t * P:t * P + (t + 1) * P]
                    pool.affine_select(out=cols, in_=cols, compare_op=ALU.is_ge, fill=NEG, base=t * P,
                                       pattern=[[-1, (t + 1) * P]], channel_multiplier=1).then_inc(mask_ready, 1)
            for t in range(2):
                for part, width in enumerate((256, 128)):
                    pool.wait_ge(ssq_mla, 2 * t + part + 1)
                    rstd(stat[:, 8 + 2 * t + part:9 + 2 * t + part], stat[:, 4 + 2 * t + part:5 + 2 * t + part], width).then_inc(rstd_mla, 1)
            own.link(pool.memset(maskC[:, :], 1.0))
            for t in range(2):
                cols = maskC[:, t * 16:(t + 1) * 16]
                own.link(pool.affine_select(out=cols, in_=cols, compare_op=ALU.is_ge, fill=0.0, base=t * P - 31,
                                            pattern=[[-16, 16]], channel_multiplier=1))
                own.link(pool.iota(biasC[:, t * P:t * P + 16], [[-16, 16]], base=t * P - 31, channel_multiplier=1,
                                   allow_small_or_imprecise_dtypes=True))
                for h in range(NH - 1, -1, -1):
                    cols = biasC[:, t * P + h * 16:t * P + (h + 1) * 16]
                    own.link(pool.tensor_scalar(out=cols, in0=biasC[:, t * P:t * P + 16], scalar1=-(2.0 ** -(h + 1)), scalar2=None, op0=ALU.mult))
                    own.link(pool.affine_select(out=cols, in_=cols, compare_op=ALU.is_ge, fill=NEG, base=t * P - 31,
                                                pattern=[[-16, 16]], channel_multiplier=1))
            own.link(pool.memset(blkmask[:, :], 1.0))
            own.link(pool.affine_select(out=blkmask[:, :], in_=blkmask[:, :], compare_op=ALU.is_ge, fill=0.0, base=0,
                                        pattern=[[-16, 8]], channel_multiplier=1))
            own.link(pool.affine_select(out=blkmask[:, :], in_=blkmask[:, :], compare_op=ALU.is_ge, fill=0.0, base=15,
                                        pattern=[[16, 8]], channel_multiplier=-1))
            pool.engine_nop().then_inc(mask_ready, 1)

            def rstd_h(t):
                pool.wait_ge(ssq2, 2 * t + 2)
                own.link(pool.tensor_tensor(out=stat[:, 16 + t:17 + t], in0=stat[:, 32 + 2 * t:33 + 2 * t],
                                            in1=stat[:, 33 + 2 * t:34 + 2 * t], op=ALU.add))
                rstd(stat[:, 18 + t:19 + t], stat[:, 16 + t:17 + t], DM).then_inc(rstd2, 1)

            rstd_h(0)

            def take(t, s):
                pool.wait_ge(chosen_ready, s + 1)
                pool.sem_inc(pass_pool, 1)
                pool.tensor_copy(idx_dn[t][:, :], chosen[t][:, :]).then_inc(chosen_taken, 1)
                pool.wait_ge(chosen_taken, s + 1)
                pool.sem_inc(pass_pool, 1)

            def keep(t):
                own.link(pool.tensor_copy(idx_up[t][:, :], idx_dn[t][:, :]))
                pool.sem_inc(pass_pool, 1)

            def gather(ring, arrived, used, table, idx, k, s, first):
                if not (first and k < RING):
                    pool.wait_ge(used, s * SLOTS + k - RING + 1)
                    pool.sem_inc(pass_pool, 1)
                pool.indirect_dma_start(
                    out=ring[:, k % RING, :], out_offset=None, in_=table,
                    in_offset=bass.IndirectOffsetOnAxis(ap=idx[:, k:k + 1], axis=0)).then_inc(arrived[k % RING], 16)

            def down(t, k, s, first=False):
                gather(ring_dn, dn_in, dn_used, a["expert_down"], idx_dn[t], k, s, first)

            def up(t, k, s, first=False):
                gather(ring_up, up_in, up_used, a["expert_up"], idx_up[t], k, s, first)

            take(0, 0)
            pool.wait_ge(y_mm, 6)
            for k in range(SLOTS):
                if k == RING // 2:
                    pool.wait_ge(y_mm, 8)
                down(0, k, 0, first=True)
            rstd_h(1)
            pool.wait_ge(wo_mm, 4)
            keep(0)
            for k in range(SLOTS):
                up(0, k, 0, first=True)
            take(1, 1)
            for k in range(SLOTS):
                down(1, k, 1)
            keep(1)
            for k in range(RING):
                up(1, k, 1)
            take(0, 2)
            for k in range(SLOTS):
                down(0, k, 2)
                if k >= SLOTS - RING:
                    up(1, k, 1)
            n0 = own.n
            with pool.Fori(1, LOOPS) as i:
                own.turn = (i - 1) * 2
                own.n = n0
                keep(0)
                take(1, 2 * i + 1)
                for k in range(SLOTS):
                    down(1, k, 2 * i + 1)
                    up(0, k, 2 * i)
                keep(1)
                take(0, 2 * i + 2)
                for k in range(SLOTS):
                    down(0, k, 2 * i + 2)
                    up(1, k, 2 * i + 1)
            own.turn, own.n = 0, n0 + 2 * (LOOPS - 1)
            keep(0)
            take(1, LAST)
            for k in range(SLOTS):
                down(1, k, LAST)
                up(0, k, LAST - 1)
            keep(1)

            for k in range(SLOTS):
                if k == 10:
                    pool.wait_ge(ssq3, 1)
                    rstd(stat[:, 26:27], stat[:, 24:25], DM).then_inc(rstd3, 1)
                up(1, k, LAST)
            pool.wait_ge(ssq3, 3)
            own.link(pool.tensor_tensor(out=stat[:, 25:26], in0=stat[:, 28:29], in1=stat[:, 29:30], op=ALU.add))
            rstd(stat[:, 27:28], stat[:, 25:26], DM).then_inc(rstd3, 1)

        @block.scalar
        def _(act):
            own = Steps(act, own_act)

            def copy(out_, in_, scale=1.0):
                return act.activation(out_, in_, ACT.Copy, scale=scale)

            act.wait_ge(x_in[1], 16)
            act.activation(gt[:, 1, DM:2 * DM], xs[:, 1, :], ACT.Square, accum_out=stat[:, 1:2]).then_inc(ssq[1], 1)
            act.dma_start(gmc[:, 0:2], a["mla_q_norm_g"].rearrange("o (k p) -> p (o k)", p=P), allow_slow_non_contiguous=True).then_inc(vec_in, 16)
            act.dma_start(gmc[:, 2:3], a["mla_kv_norm_g"].rearrange("o (k p) -> p (o k)", p=P), allow_slow_non_contiguous=True).then_inc(vec_in, 16)
            act.dma_start(pos_i32[:, :], a["positions"].rearrange("o (t p) -> p (o t)", p=P), allow_slow_non_contiguous=True).then_inc(pos_in, 16)
            for n, name in enumerate(("sub_keys_1", "sub_keys_2")):
                act.dma_start(sk_in[:, n * P:(n + 1) * P], a[name]).then_inc(sk_sem, 16)
            for v, name in enumerate(("pos_k", "pos_v")):
                for half in range(2):
                    act.dma_start(pos_row[half * HD:(half + 1) * HD, v, :],
                                   a[name].rearrange("(l h) d -> h d l", h=2)[half], allow_slow_non_contiguous=True).then_inc(pos_in, 16)
            def a_unit(u, dst, cols=None, scale=1.0):
                act.wait_ge(a_mm, u + 1)
                w = cols or dst.shape[-1]
                return copy(dst, banks[6 + u % 2][:, 0:w], scale)

            for t in range(2):
                a_unit(t, mla_tok[:, t, :]).then_inc(a_cp, 1)
            act.wait_ge(a_cp, 2)
            for t in range(2):
                act.activation(rope[:, t, 0:8, :], mla_tok[:, t, 0:256].rearrange("p (a b) -> p a b", a=8), ACT.Square,
                               accum_out=stat[:, 4 + 2 * t:5 + 2 * t]).then_inc(ssq_mla, 1)
                act.activation(rope[:, t, 8:12, :], mla_tok[:, t, 256:384].rearrange("p (a b) -> p a b", a=4), ACT.Square,
                               accum_out=stat[:, 5 + 2 * t:6 + 2 * t]).then_inc(ssq_mla, 1)
            a_unit(2, kvc[0]).then_inc(a_cp, 1)
            a_unit(3, kvc[1]).then_inc(a_cp, 1)
            a_unit(4, keyT[0]).then_inc(a_cp, 1)
            for t in range(2):
                a_unit(5 + t, val[0][:, t, :]).then_inc(a_cp, 1)
            a_unit(7, keyT[1]).then_inc(a_cp, 1)
            for t in range(2):
                a_unit(8 + t, val[1][:, t, :], P)
                act.activation(nsag[:, t * 24:(t + 1) * 24], banks[6 + (8 + t) % 2][:, P:P + 24], ACT.Tanh, scale=0.5).then_inc(a_cp, 1)
            act.wait_ge(ang_ready, 1)
            act.activation(trig[:, :, :, :], view_trig_in(ang), ACT.Sin).then_inc(trig_ready, 1)
            act.wait_ge(sk_mm, 1)
            copy(skT[:, :], banks[3][:, 0:256]).then_inc(sk_cp, 1)

            mla_scale = float(np.float32(QKW ** -0.5))
            for b in range(2):
                act.wait_ge(j_mm, b + 1)
                copy(qnT[:, 2 * b:2 * b + 2, :], banks[b][:, :].rearrange("p (a b) -> p a b", a=2), mla_scale).then_inc(j_act, 1)
            for n, b in enumerate((5, 2)):
                act.wait_ge(j_mm, 4 + n)
                copy(knT[:, 2 * n:2 * n + 2, :], banks[b][:, :].rearrange("p (a b) -> p a b", a=2)).then_inc(j_act, 1)
            for j in range(4):
                a_unit(10 + j, qT[:, j, :], scale=HD ** -0.5).then_inc(a_cp, 1)
            for t, b in enumerate((1, 4)):
                act.wait_ge(pe_mm, t + 1)
                src = banks[b][:, 0:384].rearrange("p (a b) -> p a b", a=3)
                copy(peT[:, 0:2, tok_rows[t]], src[:, 0:2, :], mla_scale)
                copy(peT[:, 2, tok_rows[t]], src[:, 2, :]).then_inc(pe_cp, 1)
            act.wait_ge(hid_u, 1)
            act.activation(cmpw[:, 2, :], cmpw[:, 1, :], ACT.Tanh, scale=GELU_S).then_inc(hid_t, 1)
            gate_tanh(act, 0)
            act.wait_ge(kc_mm, 2)
            copy(kcT[:, :], banks[2][:, 0:32]).then_inc(kc_cp, 1)
            for t in range(2):
                act.wait_ge(sc_max, t + 1)
                act.activation(Sc[:, t * P:(t + 1) * P], Sc[:, t * P:(t + 1) * P], ACT.Exp).then_inc(sc_exp, 1)
            gate_tanh(act, 1)
            done = 2
            for n, (kind, t, j) in enumerate(UNITS):
                act.wait_ge(s_max, n + 1)
                if n >= 2:
                    act.wait_ge(pt_mm, n - 1)
                K = (t + 1) * P
                for e, h in enumerate(heads(kind, j)):
                    at_sum = (n // 4) * 8 + h
                    act.activation(P_sb[n % 2][:, e, 0:K], S_sb[n % 2][:, e, 0:K], ACT.Exp,
                                   bias=mxs[:, 4 * (n % 2) + 2 + e:4 * (n % 2) + 3 + e],
                                   accum_out=sums[:, at_sum:at_sum + 1]).then_inc(p_ready, 1)
                while KC * (done + 1) <= gate_upto(n - 1):
                    gate_tanh(act, done)
                    done += 1
            while done < 8:
                gate_tanh(act, done)
                done += 1
            for b in range(4):
                act.wait_ge(ot_mm, b + 1)
                t, part = b % 2, b // 2
                copy(oTv[:, 4 * part:4 * part + 4, tok_rows[t]], banks[b][:, :].rearrange("p (a b) -> p a b", a=4)).then_inc(ot_cp, 1)
            def mergedT_copy(t):
                for half in range(2):
                    act.wait_ge(mg_mm, 2 * t + half + 1)
                    copy(xTv[:, 4 * half:4 * half + 4, tok_rows[t]],
                         banks[mg_bank(t, half)][:, :].rearrange("p (a b) -> p a b", a=4)).then_inc(mg_cp, 1)

            def square_h(t):
                for half in range(2):
                    act.wait_ge(h_ready, 2 * t + half + 1)
                    at_sum = 32 + 2 * t + half
                    act.activation(normed(t, half), xs[:, t, cols[half]], ACT.Square, accum_out=stat[:, at_sum:at_sum + 1]).then_inc(ssq2, 1)

            def normedT_copy(t):
                for half in range(2):
                    act.wait_ge(xt2_mm, 2 * t + half + 1)
                    copy(oTv[:, 4 * half:4 * half + 4, tok_rows[t]],
                         banks[xt2_bank(t, half)][:, :].rearrange("p (a b) -> p a b", a=4)).then_inc(xt2_cp, 1)

            def query_copy(t, p):
                act.wait_ge(q_mm, p + 1)
                copy(q_tok[t], banks[4][:, t * 256:(t + 1) * 256]).then_inc(q_cp, 1)

            def queryT_copy(t, p):
                act.wait_ge(qt_mm, p + 1)
                copy(q_T[t], banks[5][:, t * 256:(t + 1) * 256]).then_inc(qt_cp, 1)

            def softmax_exp(t, p):
                act.wait_ge(top_ready, p + 1)
                act.activation(soft[t], ts_v, ACT.Exp, bias=d_stat[:, 0:1], accum_out=d_stat[:, 1:2]).then_inc(exp_ready, 1)

            def gelu_tanh(s):
                act.wait_ge(poly_ready, s + 1)
                act.activation(gel[:, 1, :], gel[:, 0, :], ACT.Tanh, scale=GELU_S).then_inc(tanh_ready, 1)

            def diagonal(t, k, s, first=False):
                if k == 0:
                    act.wait_ge(cof_ready, s + 1)
                if not (first and k < RING):
                    act.wait_ge(up_used, s * SLOTS + k - RING + 1)
                act.activation(diag[:, k % RING, :], ident[:, :], ACT.Copy, scale=cof[t][:, k:k + 1]).then_inc(diag_ready, 1)

            def half_step(t_up, s, prepare):
                if prepare:
                    query_copy(t_up, s + 2)
                for k in range(SLOTS):
                    if k == 4 and prepare:
                        queryT_copy(t_up, s + 2)
                    if k == 12 and prepare:
                        softmax_exp(t_up, s + 2)
                    diagonal(t_up, k, s)
                gelu_tanh(s + 1)

            mergedT_copy(0)
            square_h(0)
            normedT_copy(0)
            query_copy(0, 0)
            queryT_copy(0, 0)
            softmax_exp(0, 0)
            mergedT_copy(1)
            square_h(1)
            normedT_copy(1)
            gelu_tanh(0)
            act.wait_ge(y_started, 1)
            for k in range(RING):
                diagonal(0, k, 0, first=True)
            query_copy(1, 1)
            queryT_copy(1, 1)
            for k in range(RING, SLOTS):
                if k == 8:
                    softmax_exp(1, 1)
                if k == 10:
                    query_copy(0, 2)
                if k == 11:
                    queryT_copy(0, 2)
                diagonal(0, k, 0, first=True)
            softmax_exp(0, 2)
            gelu_tanh(1)
            half_step(1, 1, True)
            with act.Fori(1, LOOPS) as i:
                half_step(0, 2 * i, True)
                half_step(1, 2 * i + 1, True)
            half_step(0, LAST - 1, False)
            for k in WEIGHED:
                if k == RING:
                    act.wait_ge(hy_ready, 1)
                    act.activation(gt[:, 0, 0:DM], xs[:, 0, :], ACT.Square, accum_out=stat[:, 24:25]).then_inc(ssq3, 1)
                diagonal(1, k, LAST)
            for half in range(2):
                act.wait_ge(hy_ready, half + 2)
                act.activation(gt[:, 1, cols[half]], xs[:, 1, cols[half]], ACT.Square,
                               accum_out=stat[:, 28 + half:29 + half]).then_inc(ssq3, 1)

        @block.vector
        def _(dve):
            own = Steps(dve, own_dve)
            link = own.link

            dve.wait_ge(x_in[0], 16)
            dve.tensor_tensor_reduce(out=gt[:, 0, DM:2 * DM], in0=xs[:, 0, :], in1=xs[:, 0, :], scale=1.0, scalar=0.0,
                                     op0=ALU.mult, op1=ALU.add, accum_out=stat[:, 0:1]).then_inc(ssq[0], 1)
            for t in range(2):
                dve.wait_ge(rstd1, t + 1)
                dve.tensor_scalar(out=gt[:, t, 0:DM], in0=xs[:, t, :], scalar1=stat[:, 2 + t:3 + t], scalar2=None, op0=ALU.mult).then_inc(xn_ready, 1)
            dve.wait_ge(g1_in, 16)
            for n in range(4):
                t, half = n // 2, n % 2
                dve.wait_ge(xt_mm, n + 1)
                dve.tensor_tensor(out=xTv[:, 4 * half:4 * half + 4, tok_rows[t]],
                                  in0=banks[2 + n % 2][:, :].rearrange("p (a b) -> p a b", a=4),
                                  in1=bc(g1c[:, 4 * half:4 * half + 1], [[1, 4], [0, P]]), op=ALU.mult).then_inc(xt_cp, 1)
            for t in range(2):
                dve.wait_ge(rstd_mla, 2 * t + 2)
                dve.tensor_scalar(out=mla_tok[:, t, 0:256], in0=mla_tok[:, t, 0:256], scalar1=stat[:, 8 + 2 * t:9 + 2 * t],
                                  scalar2=None, op0=ALU.mult).then_inc(mla_scaled, 1)
                dve.tensor_scalar(out=mla_tok[:, t, 256:384], in0=mla_tok[:, t, 256:384], scalar1=stat[:, 9 + 2 * t:10 + 2 * t],
                                  scalar2=None, op0=ALU.mult).then_inc(mla_scaled, 1)
            dve.wait_ge(pos_in, 80)
            dve.wait_ge(const_ready, 1)
            link(dve.tensor_copy(stat[:, 30:32], pos_i32[:, :]))
            for t in range(2):
                dve.tensor_scalar(out=ang[:, 4, 16 * t:16 * t + 16], in0=ang[:, 0, 0:16], scalar1=stat[:, 30 + t:31 + t],
                                  scalar2=None, op0=ALU.mult).then_inc(own_dve, 1)
            own.n += 2
            dve.wait_ge(own_dve, own.n)
            two_pi = 2.0 * np.pi
            c1 = 6.28125
            c2 = float(np.float32(two_pi - c1))
            c3 = float(two_pi - c1 - c2)
            magic = 12582912.0
            link(dve.tensor_scalar(out=ang[:, 1, :], in0=ang[:, 4, :], scalar1=float(1.0 / two_pi), scalar2=None, op0=ALU.mult))
            link(dve.tensor_scalar(out=ang[:, 1, :], in0=ang[:, 1, :], scalar1=magic, scalar2=None, op0=ALU.add))
            link(dve.tensor_scalar(out=ang[:, 1, :], in0=ang[:, 1, :], scalar1=magic, scalar2=None, op0=ALU.subtract))
            for c in (c1, c2, c3):
                link(dve.scalar_tensor_tensor(out=ang[:, 4, :], in0=ang[:, 1, :], scalar=-c, in1=ang[:, 4, :], op0=ALU.mult, op1=ALU.add))
            link(dve.tensor_scalar(out=ang[:, 3, :], in0=ang[:, 4, :], scalar1=float(np.pi / 2), scalar2=None, op0=ALU.add))
            link(dve.tensor_scalar(out=ang[:, 2, :], in0=ang[:, 3, :], scalar1=float(np.pi), scalar2=two_pi, op0=ALU.is_gt, op1=ALU.mult))
            link(dve.tensor_tensor(out=ang[:, 3, :], in0=ang[:, 3, :], in1=ang[:, 2, :], op=ALU.subtract))
            dve.tensor_scalar(out=ang[:, 3:5, :], in0=ang[:, 3:5, :], scalar1=3.1415925, scalar2=-3.1415925, op0=ALU.min, op1=ALU.max).then_inc(ang_ready, 1)

            dve.wait_ge(vec_in, 32)
            for t in range(2):
                dve.wait_ge(mt_mm, t + 1)
                dve.tensor_tensor(out=mlaT[:, :, tok_rows[t]], in0=banks[2 + t][:, 0:384].rearrange("p (a b) -> p a b", a=3),
                                  in1=bc(gmc[:, 0:1], [[1, 3], [0, P]]), op=ALU.mult).then_inc(mt_cp, 1)
            dve.wait_ge(kk_in, 8 * 16)
            dve.wait_ge(mask_ready, 17)
            for v in range(2):
                for g in range(2):
                    dve.tensor_tensor(out=blk[v][:, :, 16 * g:16 * g + 15],
                                      in0=bc(kk[v][g][:, 0:1], [[2, 16], [16, 15]]),
                                      in1=bc(pos_row[:, v, 0:1], [[1, 16], [0, 15]]), op=ALU.add).then_inc(blk_ready, 1)
            dve.wait_ge(trig_ready, 1)
            dve.wait_ge(j_mm, 3)
            dve.wait_ge(ssq_mla, 4)
            for t in range(2):
                src = bc(mla_tok[:, t, 384:385], [[0, 4], [1, ROPE]])
                dve.tensor_copy(rope[:, t, 0:8, :], banks[4][:, 256 * t:256 * t + 256].rearrange("p (a b) -> p a b", a=8)).then_inc(own_dve, 1)
                dve.tensor_copy(rope[:, t, 8:12, :], src).then_inc(own_dve, 1)
                own.n += 2
                dve.wait_ge(own_dve, own.n)
                x1, x2 = rope[:, t, :, 0:16], rope[:, t, :, 16:32]
                cos = bc(trig[:, 0, t, 0:1], [[0, 12], [1, 16]])
                sin = bc(trig[:, 1, t, 0:1], [[0, 12], [1, 16]])
                dve.tensor_tensor(out=ropt[0], in0=x1, in1=sin, op=ALU.mult).then_inc(own_dve, 1)
                dve.tensor_tensor(out=ropt[1], in0=x2, in1=sin, op=ALU.mult).then_inc(own_dve, 1)
                own.n += 2
                dve.wait_ge(own_dve, own.n)
                link(dve.tensor_tensor(out=x1, in0=x1, in1=cos, op=ALU.mult))
                link(dve.tensor_tensor(out=x2, in0=x2, in1=cos, op=ALU.mult))
                dve.tensor_tensor(out=x1, in0=x1, in1=ropt[1], op=ALU.subtract).then_inc(own_dve, 1)
                dve.tensor_tensor(out=x2, in0=x2, in1=ropt[0], op=ALU.add).then_inc(own_dve, 1)
                own.n += 2
                dve.wait_ge(own_dve, own.n)
                dve.engine_nop().then_inc(roped, 1)
            for t, b in enumerate((3, 0)):
                dve.wait_ge(j_mm, 6 + t)
                dve.tensor_copy(vml[:, t, :], banks[b][:, :]).then_inc(j_dve, 1)
            dve.wait_ge(hid_mm, 1)
            link(dve.tensor_copy(cmpw[:, 0, :], banks[5][:, 0:64]))
            link(dve.tensor_tensor(out=cmpw[:, 1, :], in0=cmpw[:, 0, :], in1=cmpw[:, 0, :], op=ALU.mult))
            link(dve.tensor_scalar(out=cmpw[:, 1, :], in0=cmpw[:, 1, :], scalar1=GELU_C, scalar2=1.0, op0=ALU.mult, op1=ALU.add))
            dve.tensor_tensor(out=cmpw[:, 1, :], in0=cmpw[:, 1, :], in1=cmpw[:, 0, :], op=ALU.mult).then_inc(hid_u, 1)
            dve.wait_ge(hid_t, 1)
            link(dve.scalar_tensor_tensor(out=cmpw[:, 3, :], in0=cmpw[:, 2, :], scalar=1.0, in1=cmpw[:, 0, :], op0=ALU.add, op1=ALU.mult))
            link(dve.tensor_scalar(out=cmpw[:, 4, :], in0=cmpw[:, 3, :], scalar1=0.5, scalar2=None, op0=ALU.mult))
            dve.tensor_copy(hvrep.rearrange("p (g j n) -> p g j n", g=2, j=4),
                            bc(cmpw[:, 4, 32:33], [[16, 2], [0, 4], [1, 16]])).then_inc(hid_ready, 1)
            dve.wait_ge(kc_cp, 1)
            dve.tensor_tensor(out=VBD.rearrange("p (h d) -> p h d", h=NH), in0=bc(banks[2][:, 64:65], [[0, NH], [1, HD]]),
                              in1=bc(blkmask[:, 0:1], [[1, NH], [0, HD]]), op=ALU.mult).then_inc(vbd_ready, 1)
            dve.wait_ge(a_cp, 10)
            link(dve.tensor_scalar(out=nsag[:, :], in0=nsag[:, :], scalar1=0.5, scalar2=0.5, op0=ALU.mult, op1=ALU.add))

            def heads_scaled(dst, src, scal):
                return dve.tensor_tensor(out=dst.rearrange("p (h d) -> p h d", h=NH), in0=src.rearrange("p (h d) -> p h d", h=NH),
                                         in1=bc(scal, [[1, NH], [0, HD]]), op=ALU.mult)

            for t in range(2):
                sc = Sc[:, t * P:(t + 1) * P]
                sc3 = sc.rearrange("p (h n) -> p h n", h=NH)
                dve.wait_ge(sc_mm, t + 1)
                link(dve.tensor_tensor(out=sc, in0=banks[t][:, 0:P], in1=biasC[:, t * P:(t + 1) * P], op=ALU.add))
                link(dve.tensor_reduce(out=coef[:, 32:40], in_=sc3, axis=AXX, op=ALU.max))
                dve.tensor_tensor(out=sc3, in0=sc3, in1=bc(coef[:, 32:33], [[1, NH], [0, 16]]), op=ALU.subtract).then_inc(sc_max, 1)
                dve.wait_ge(sc_max, t + 1)
            for t in range(2):
                sc3 = Sc[:, t * P:(t + 1) * P].rearrange("p (h n) -> p h n", h=NH)
                dve.wait_ge(sc_exp, t + 1)
                link(dve.tensor_tensor(out=sc3, in0=sc3, in1=bc(maskC[:, 16 * t:16 * t + 1], [[0, NH], [1, 16]]), op=ALU.mult))
                dve.engine_nop().then_inc(pc_ready, 1)
                cc = coef[:, 8 * t:8 * t + 8]
                link(dve.tensor_reduce(out=cc, in_=sc3, axis=AXX, op=ALU.add))
                link(dve.tensor_scalar(out=cc, in0=cc, scalar1=1e-30, scalar2=None, op0=ALU.max))
                link(dve.reciprocal(cc, cc))
                link(dve.tensor_tensor(out=cc, in0=cc, in1=nsag[:, 24 * t:24 * t + 8], op=ALU.mult))
            for t in range(2):
                dve.wait_ge(ptc_mm, 2)
                dve.tensor_copy(PTc[:, t * P:(t + 1) * P], banks[3][:, t * P:(t + 1) * P]).then_inc(ptc_cp, 1)
            for t in range(2):
                dve.wait_ge(oc_mm, t + 1)
                heads_scaled(o_nsa[t], banks[4 + t][:, :], coef[:, 8 * t:8 * t + 1]).then_inc(oc_done, 1)
            dve.wait_ge(oc_done, 2)

            def combine(gi):
                kind, t, _ = UNITS[4 * gi]
                dve.wait_ge(pv_mm, 4 * gi + 4)
                cc = coef[:, 48:56]
                link(dve.reciprocal(cc, sums[:, 8 * gi:8 * gi + 8]))
                if kind == "mla":
                    heads_scaled(o_tmp if t == 0 else o_mla1[:, :], banks[4 + gi % 2][:, :], coef[:, 48:49]).then_inc(o_done, 1)
                    return
                which = 1 if kind == "sel" else 2
                link(dve.tensor_tensor(out=cc, in0=cc, in1=nsag[:, 24 * t + 8 * which:24 * t + 8 * which + 8], op=ALU.mult))
                link(heads_scaled(o_tmp, banks[4 + gi % 2][:, :], coef[:, 48:49]))
                dve.tensor_tensor(out=o_nsa[t], in0=o_nsa[t], in1=o_tmp, op=ALU.add).then_inc(o_done, 1)
                dve.wait_ge(o_done, gi + 1)

            N = len(UNITS)
            for n in range(N + 3):
                if 2 <= n < N + 2:
                    m = n - 2
                    w = 2 * (UNITS[m][1] + 1) * P
                    dve.wait_ge(pt_mm, m + 1)
                    if m >= 2:
                        dve.wait_ge(pv_mm, m - 1)
                    dve.tensor_copy(PT_sb[m % 2][:, 0:w], banks[2 + m % 2][:, 0:w]).then_inc(pt_cp, 1)
                if n < N:
                    kind, t, j = UNITS[n]
                    K = (t + 1) * P
                    dve.wait_ge(s_mm, n + 1)
                    if n >= 2:
                        dve.wait_ge(p_ready, 2 * (n - 1))
                    for e, h in enumerate(heads(kind, j)):
                        bias = maskM[:, t * P:t * P + K] if kind == "mla" else biasN[:, h, t * P:t * P + K]
                        m = 4 * (n % 2) + e
                        dve.tensor_tensor_reduce(out=S_sb[n % 2][:, e, 0:K], in0=banks[n % 2][:, e * K:(e + 1) * K], in1=bias,
                                                 scale=1.0, scalar=LOWEST, op0=ALU.add, op1=ALU.max, accum_out=mxs[:, m:m + 1]).then_inc(own_dve, 1)
                        own.n += 1
                    dve.wait_ge(own_dve, own.n)
                    m = 4 * (n % 2)
                    dve.tensor_scalar(out=mxs[:, m + 2:m + 4], in0=mxs[:, m:m + 2], scalar1=-1.0, scalar2=None, op0=ALU.mult).then_inc(s_max, 1)
                if n >= 6 and (n - 6) % 4 == 0:
                    combine((n - 6) // 4)
            dve.wait_ge(a_cp, 22)
            for t in range(2):
                link(dve.tensor_scalar(out=gt[:, t, :], in0=gt[:, t, :], scalar1=0.5, scalar2=0.5, op0=ALU.mult, op1=ALU.add))
            def gated(t, n):
                dve.wait_ge(y_mm, 4 * t + n + 1)
                part = gt[:, t, n * 512:(n + 1) * 512]
                dve.tensor_tensor(out=part, in0=part, in1=banks[y_bank(t, n)][:, :], op=ALU.mult).then_inc(y_used, 1)

            def merge(t, half):
                dve.wait_ge(y_used, 4 * t + half + 3)
                part = gt[:, t, cols[half]]
                dve.tensor_tensor(out=part, in0=part, in1=normed(t, half), op=ALU.add).then_inc(merged, 1)

            def residual(t):
                for half in range(2):
                    dve.wait_ge(wo_mm, 2 * t + half + 1)
                    part = xs[:, t, cols[half]]
                    dve.tensor_tensor(out=part, in0=part, in1=banks[wo_bank(t, half)][:, :], op=ALU.add).then_inc(h_ready, 1)

            def norm2(t):
                dve.wait_ge(rstd2, t + 1)
                for half in range(2):
                    dve.scalar_tensor_tensor(out=normed(t, half), in0=xs[:, t, cols[half]], scalar=stat[:, 18 + t:19 + t],
                                             in1=g2b[:, cols[half]], op0=ALU.mult, op1=ALU.mult).then_inc(xt2_ready, 1)

            for n in range(3):
                gated(0, n)
            merge(0, 0)
            gated(0, 3)
            merge(0, 1)
            dve.wait_ge(g2_in, 16)
            residual(0)
            norm2(0)
            gated(1, 0)

            def top16(*searches):
                def then(make):
                    for search in searches:
                        own.mark(make(*search))
                    ready()

                def ready():
                    own.wait()
                    dve.sem_inc(pass_dve, 1)
                then(lambda values, index, src, scratch: dve.max(values[:, 0:8], src))
                for values, index, src, scratch in searches:
                    own.mark(dve.match_replace(scratch, values[:, 0:8], src, LOWEST))
                for values, index, src, scratch in searches:
                    dve.max_index(index[:, 0:8], values[:, 0:8], src)
                ready()
                then(lambda values, index, src, scratch: dve.max(values[:, 8:16], scratch))
                then(lambda values, index, src, scratch: dve.max_index(index[:, 8:16], values[:, 8:16], scratch))

            def choose(t, p):
                dve.wait_ge(key_mm, p + 1)
                dve.sem_inc(pass_dve, 1)
                top16(*[(top_v[:, half, :], top_i[:, half * TOP:(half + 1) * TOP],
                         banks[6][:, t * 256 + half * NK:t * 256 + (half + 1) * NK], scrap[:, half * NK:(half + 1) * NK])
                        for half in range(2)])
                dve.tensor_copy(top_if.rearrange("p a b -> p (a b)"), top_i[:, :]).then_inc(keys_read, 1)
                link(dve.tensor_tensor(out=cand.rearrange("p (a b) -> p a b", a=TOP), in0=bc(top_v[:, 0, 0:1], [[1, TOP], [0, TOP]]),
                                       in1=bc(top_v[:, 1, 0:1], [[0, TOP], [1, TOP]]), op=ALU.add))
                dve.sem_inc(pass_dve, 1)
                top16((ts_v, pos_i, cand, scrap2))
                dve.tensor_scalar(out=d_stat[:, 0:1], in0=ts_v[:, 0:1], scalar1=-1.0, scalar2=None, op0=ALU.mult).then_inc(top_ready, 1)
                dve.tensor_scalar(out=ab_i[:, 0:TOP], in0=pos_i[:, :], scalar1=4, scalar2=None, op0=ALU.logical_shift_right)
                link(dve.tensor_scalar(out=ab_i[:, TOP:2 * TOP], in0=pos_i[:, :], scalar1=15, scalar2=None, op0=ALU.bitwise_and))
                link(dve.tensor_copy(ab_f.rearrange("p a b -> p (a b)"), ab_i[:, :]))
                link(dve.tensor_tensor(out=hot.rearrange("p (h a b) -> p h a b", h=2, a=TOP), in0=bc(ab_f[:, 0, 0:1], [[TOP, 2], [1, TOP], [0, TOP]]),
                                       in1=bc(io16[:, 0:1], [[0, 2], [0, TOP], [1, TOP]]), op=ALU.is_equal))
                link(dve.tensor_tensor(out=hot.rearrange("p (h a b) -> p h a b", h=2, a=TOP), in0=hot.rearrange("p (h a b) -> p h a b", h=2, a=TOP),
                                       in1=bc(top_if[:, 0, 0:1], [[TOP, 2], [0, TOP], [1, TOP]]), op=ALU.mult))
                link(dve.tensor_reduce(out=r12.rearrange("p h a -> p (h a)"), in_=hot.rearrange("p (q b) -> p q b", b=TOP), axis=AXX, op=ALU.add))

            def give(t, p, first=False):
                if not first:
                    dve.wait_ge(chosen_taken, p - 1)
                dve.scalar_tensor_tensor(out=chosen[t][:, :], in0=r12[:, 0, :], scalar=float(NK), in1=r12[:, 1, :],
                                         op0=ALU.mult, op1=ALU.add).then_inc(chosen_ready, 1)

            def softmax(t, p):
                dve.wait_ge(exp_ready, p + 1)
                link(dve.reciprocal(d_stat[:, 2:3], d_stat[:, 1:2]))
                link(dve.tensor_scalar(out=soft[t], in0=soft[t], scalar1=d_stat[:, 2:3], scalar2=0.5, op0=ALU.mult, op1=ALU.mult))

            def dot(t, k, s):
                dve.wait_ge(dn_in[k % RING], (2 * s + k // RING + 1) * 16)
                row = ring_dn[:, k % RING, :]
                dve.tensor_tensor_reduce(out=row, in0=row, in1=gt[:, t, DM:2 * DM], scale=1.0, scalar=0.0,
                                         op0=ALU.mult, op1=ALU.add, accum_out=hdn[:, k:k + 1]).then_inc(dn_used, 1)

            def coefficients(t, s, first=False):
                dve.wait_ge(dn_used, (s + 1) * SLOTS)
                link(dve.tensor_tensor(out=gel[:, 0, :], in0=hdn, in1=hdn, op=ALU.mult))
                link(dve.tensor_scalar(out=gel[:, 0, :], in0=gel[:, 0, :], scalar1=GELU_C, scalar2=1.0, op0=ALU.mult, op1=ALU.add))
                dve.tensor_tensor(out=gel[:, 0, :], in0=gel[:, 0, :], in1=hdn, op=ALU.mult).then_inc(poly_ready, 1)
                dve.wait_ge(tanh_ready, s + 1)
                link(dve.scalar_tensor_tensor(out=gel[:, 2, :], in0=gel[:, 1, :], scalar=1.0, in1=hdn, op0=ALU.add, op1=ALU.mult))
                if not first:
                    dve.wait_ge(diag_ready, (s - 1) * SLOTS)
                dve.tensor_tensor(out=cof[t], in0=gel[:, 2, :], in1=soft[t], op=ALU.mult).then_inc(cof_ready, 1)

            def half_step(t_dot, s, prepare, first=False):
                for k in range(SLOTS):
                    dot(t_dot, k, s)
                    if k == RING - 1 and prepare:
                        choose(1 - t_dot, s + 1)
                        give(1 - t_dot, s + 1)
                coefficients(t_dot, s, first)
                if prepare:
                    softmax(1 - t_dot, s + 1)

            choose(0, 0)
            give(0, 0, first=True)
            softmax(0, 0)
            for n in range(1, 4):
                gated(1, n)
            for half in range(2):
                merge(1, half)
            dve.memset(diag[:, :, :], 0.0).then_inc(y_zero, 1)
            for k in range(SLOTS):
                if k == 10:
                    residual(1)
                if k == 12:
                    norm2(1)
                dot(0, k, 0)
            coefficients(0, 0, first=True)
            choose(1, 1)
            give(1, 1, first=True)
            softmax(1, 1)
            half_step(1, 1, True, first=True)
            half_step(0, 2, True)
            n0 = own.n
            per = None
            with dve.Fori(1, LOOPS) as i:
                own.turn = (i - 1) * DVE_LINKS
                half_step(1, 2 * i + 1, True)
                half_step(0, 2 * i + 2, True)
            per = own.n - n0
            assert per == DVE_LINKS, per
            own.turn, own.n = 0, n0 + DVE_LINKS * (LOOPS - 1)
            half_step(1, LAST, False)
            dve.wait_ge(gf_in, 16)

            def add_y(t):
                dve.wait_ge(y_done, t + 1)
                for half in range(2):
                    part = xs[:, t, half * 512:(half + 1) * 512]
                    dve.tensor_tensor(out=part, in0=part, in1=banks[2 * t + half][:, :], op=ALU.add).then_inc(own_dve, 1)
                own.n += 2
                dve.wait_ge(own_dve, own.n)

            def add_row(k, at=slice(0, DM)):
                return dve.scalar_tensor_tensor(out=xs[:, 1, at], in0=ring_up[:, k % RING, at], scalar=cof[1][:, k:k + 1],
                                                in1=xs[:, 1, at], op0=ALU.mult, op1=ALU.add)

            def norm_f(t, at=slice(0, DM)):
                dve.scalar_tensor_tensor(out=xs[:, t, at], in0=xs[:, t, at], scalar=stat[:, 26 + t:27 + t], in1=gfb[:, at],
                                         op0=ALU.mult, op1=ALU.mult).then_inc(out_ready, 1)

            add_y(0)
            dve.engine_nop().then_inc(hy_ready, 1)
            dve.wait_ge(rstd3, 1)
            norm_f(0)
            dve.wait_ge(cof_ready, LAST + 1)
            for k in ADDED[:-1]:
                dve.wait_ge(up_in[k % RING], (2 * LAST + 1 + k // RING) * 16)
                link(add_row(k))
            add_y(1)
            k = ADDED[-1]
            dve.wait_ge(up_in[k % RING], (2 * LAST + 1 + k // RING) * 16)
            for half in range(2):
                add_row(k, cols[half]).then_inc(hy_ready, 1)
            dve.wait_ge(rstd3, 2)
            for half in range(2):
                norm_f(1, cols[half])

        @block.tensor
        def _(pe):
            idn = ident[:, :]

            def mm(out_, lhsT, rhs, start=True, stop=True):
                return pe.matmul(out_, lhsT, rhs, start=start, stop=stop)

            own = Steps(pe, own_pe)

            def tr(out_, in_):
                return pe.transpose(out_, in_, idn)

            pe.wait_ge(id_ready, 1)
            for n in range(4):
                t, half = n // 2, n % 2
                pe.wait_ge(xn_ready, t + 1)
                if n >= 2:
                    pe.wait_ge(xt_cp, n - 1)
                for k in range(4):
                    last = tr(banks[2 + n % 2][:, k * P:(k + 1) * P], gt[:, t, (4 * half + k) * P:(4 * half + k + 1) * P])
                last.then_inc(xt_mm, 1)

            unit = [0]

            def a_bank():
                u = unit[0]
                if u >= 2:
                    pe.wait_ge(a_cp, u - 1)
                unit[0] += 1
                return banks[6 + u % 2]

            def transposed(w, rows):
                b = a_bank()
                for k in range(KC):
                    last = mm(b[:, 0:TOK], rows(w[:, k, :]), xTv[:, k, :], k == 0, k == KC - 1)
                return last.then_inc(a_mm, 1)

            def by_token(w, t, c0, n):
                b = a_bank()
                for k in range(KC):
                    last = mm(b[:, 0:n], xTv[:, k, tok_rows[t]], w[:, k, c0:c0 + n], k == 0, k == KC - 1)
                return last.then_inc(a_mm, 1)

            def arrived(c):
                pe.wait_ge(win_in[c % 2], 16 * (c // 2 + (0 if c % 2 and c > 3 else 1)))

            gate_done = [0]

            def gate_step(upto):
                while gate_done[0] < upto:
                    m = gate_done[0]
                    v, k = m // KC, m % KC
                    c, t = v // 2, v % 2
                    if k == 0:
                        if t == 0:
                            arrived(4 + c)
                        a_bank()
                    last = mm(banks[6 + v % 2][:, :], xTv[:, k, tok_rows[t]], chunk(4 + c)[:, k, :], k == 0, k == KC - 1)
                    if k == KC - 1:
                        last.then_inc(a_mm, 1)
                    gate_done[0] += 1

            arrived(0)
            for t in range(2):
                pe.wait_ge(xt_cp, 2 * t + 2)
                by_token(chunk(0), t, 0, MLA_W)
            arrived(1)
            for b in range(3):
                transposed(chunk(1), lambda w, b=b: w[:, b * P:(b + 1) * P])
            for t in range(2):
                by_token(chunk(1), t, 384, P)
            for t in range(2):
                pe.wait_ge(mla_scaled, 2 * t + 2)
                for b in range(3):
                    last = tr(banks[2 + t][:, b * P:(b + 1) * P], mla_tok[:, t, b * P:(b + 1) * P])
                last.then_inc(mt_mm, 1)
            arrived(2)
            transposed(chunk(2), lambda w: w[:, 0:P])
            for t in range(2):
                by_token(chunk(2), t, P, P + 24)
            pe.wait_ge(sk_sem, 32)
            pe.wait_ge(mt_cp, 2)
            for n in range(2):
                last = tr(banks[3][:, n * P:(n + 1) * P], sk_in[:, n * P:(n + 1) * P])
            last.then_inc(sk_mm, 1)
            pe.wait_ge(mla_w_in, 96)
            for b in range(2):
                for e in range(2):
                    pr = 2 * b + e
                    for k in range(2):
                        last = mm(banks[b][:, e * 256:(e + 1) * 256], w_uqn[:, k, pr * P:(pr + 1) * P], mlaT[:, k, :], k == 0, k == 1)
                last.then_inc(j_mm, 1)
            for t in range(2):
                for k in range(2):
                    last = mm(banks[4][:, t * 256:(t + 1) * 256], mlaT[:, k, tok_rows[t]], w_uqp[:, k, :], k == 0, k == 1)
            last.then_inc(j_mm, 1)
            for n, b in enumerate((5, 2)):
                for e in range(2):
                    pr = 2 * n + e
                    last = mm(banks[b][:, e * 256:(e + 1) * 256], w_uk[:, pr * P:(pr + 1) * P], mlaT[:, 2, :])
                last.then_inc(j_mm, 1)
            for t, b in enumerate((3, 0)):
                if t == 1:
                    pe.wait_ge(j_act, 1)
                else:
                    pe.wait_ge(sk_cp, 1)
                mm(banks[b][:, :], mlaT[:, 2, tok_rows[t]], w_uv).then_inc(j_mm, 1)
            pe.wait_ge(win_q_in, 16 * 2 * KC)
            for j in range(4):
                transposed(chunk(3), lambda w, j=j: w[:, j * P:(j + 1) * P])
            for t, b in enumerate((1, 4)):
                pe.wait_ge(roped, 2 if t else 1)
                if t == 0:
                    pe.wait_ge(j_act, 2)
                for c in range(3):
                    last = tr(banks[b][:, c * P:(c + 1) * P], rope[:, t, 4 * c:4 * c + 4, :].rearrange("p a b -> p (a b)"))
                last.then_inc(pe_mm, 1)
            pe.wait_ge(blk_ready, 4)
            pe.wait_ge(cmp_w_in, 80)
            pe.wait_ge(j_act, 3)
            for v in range(2):
                for l in range(16):
                    last = mm(banks[5][:, 32 * v:32 * v + 32], w1[v][:, l, :], blk[v][:, l, :], l == 0, l == 15)
                    if l % 4 == 1:
                        gate_step(4 * v + l // 4 + 1)
            last.then_inc(hid_mm, 1)
            gate_step(GATE_HID)
            pe.wait_ge(hid_ready, 1)
            pe.wait_ge(j_act, 4)
            mm(banks[2][:, 0:32], w2kd, cmpw[:, 4, 0:32]).then_inc(kc_mm, 1)
            mm(banks[2][:, 64:128], hvrep, w2v).then_inc(kc_mm, 1)
            gate_step(GATE_HID + 1)
            pe.wait_ge(kc_cp, 1)
            pe.wait_ge(j_dve, 2)
            for t in range(2):
                if t == 1:
                    pe.wait_ge(pe_cp, 1)
                for h in range(NH):
                    g, j = h // 4, h % 4
                    rows = slice(g * HD, (g + 1) * HD)
                    last = mm(banks[t][:, h * 16:(h + 1) * 16], qT[rows, j, tok_rows[t]], kcT[rows, 16 * g:16 * g + 16])
                    if h == 3:
                        own.mark(last)
                        gate_step(GATE_HID + 2 + t)
                        own.wait()
                last.then_inc(sc_mm, 1)
            gate_step(GATE_CMP)
            for t in range(2):
                pe.wait_ge(pc_ready, t + 1)
                tr(banks[3][:, t * P:(t + 1) * P], Sc[:, t * P:(t + 1) * P]).then_inc(ptc_mm, 1)
            gate_step(GATE_PRE)
            pe.wait_ge(vbd_ready, 1)
            pe.wait_ge(pe_cp, 2)
            for t in range(2):
                pe.wait_ge(ptc_cp, t + 1)
                mm(banks[4 + t][:, :], PTc[:, t * P:(t + 1) * P], VBD).then_inc(oc_mm, 1)

            def scores(n):
                kind, t, j = UNITS[n]
                K = (t + 1) * P
                if n < 2:
                    pe.wait_ge(sc_max, 2)
                else:
                    pe.wait_ge(s_max, n - 1)
                for e, h in enumerate(heads(kind, j)):
                    dst = banks[n % 2][:, e * K:(e + 1) * K]
                    rows = slice(e * HD, (e + 1) * HD)
                    if e:
                        yield own.mark(last)
                        own.wait()
                    if kind == "mla":
                        quad = slice(32 * (h % 4), 32 * (h % 4) + 32)
                        yield own.mark(mm(dst, qnT[rows, j, tok_rows[t]], knT[rows, j, 0:K], True, False))
                        own.wait()
                        last = pe.matmul(dst, peT[quad, h // 4, tok_rows[t]], peT[quad, 2, 0:K], start=False, stop=True,
                                         tile_position=(32 * (h % 4), 0))
                    else:
                        last = mm(dst, qT[rows, j, tok_rows[t]], keyT[0 if kind == "sel" else 1][rows, 0:K])
                last.then_inc(s_mm, 1)

            def turn(n):
                t = UNITS[n][1]
                pe.wait_ge(p_ready, 2 * n + 2)
                if n >= 2:
                    pe.wait_ge(pt_cp, n - 1)
                elif n == 1:
                    pe.wait_ge(ptc_cp, 2)
                for e in range(2):
                    for c in range(t + 1):
                        at_ = (e * (t + 1) + c) * P
                        last = tr(banks[2 + n % 2][:, at_:at_ + P], P_sb[n % 2][:, e, c * P:(c + 1) * P])
                last.then_inc(pt_mm, 1)

            def values(n):
                kind, t, j = UNITS[n]
                gi = n // 4
                pe.wait_ge(pt_cp, n + 1)
                if n % 4 == 0:
                    if gi < 2:
                        pe.wait_ge(oc_done, gi + 1)
                    else:
                        pe.wait_ge(o_done, gi - 1)
                for e, h in enumerate(heads(kind, j)):
                    for c in range(t + 1):
                        at_ = (e * (t + 1) + c) * P
                        if kind == "mla":
                            v = vml[:, c, h * HD:(h + 1) * HD]
                        else:
                            v = val[0 if kind == "sel" else 1][:, c, e * HD:(e + 1) * HD]
                        last = mm(banks[4 + gi % 2][:, h * HD:(h + 1) * HD], PT_sb[n % 2][:, at_:at_ + P], v, c == 0, c == t)
                last.then_inc(pv_mm, 1)

            def outputT(b):
                src = (o_nsa[0], o_nsa[1], o_tmp, o_mla1)[b]
                pe.wait_ge(o_done, b + 3)
                for k in range(4):
                    last = tr(banks[b][:, k * P:(k + 1) * P], src[:, k * P:(k + 1) * P])
                last.then_inc(ot_mm, 1)

            N = len(UNITS)
            pe.wait_ge(a_cp, 14)
            pe.wait_ge(j_dve, 2)
            pe.wait_ge(mask_ready, 17)
            for n in range(N + 3):
                work = []
                if 2 <= n < N + 2:
                    work.append(lambda: turn(n - 2))
                if n >= 3:
                    work.append(lambda: values(n - 3))
                work.append(lambda: gate_step(gate_upto(n)))
                if n < N:
                    for _ in scores(n):
                        if work:
                            work.pop(0)()
                for rest in work:
                    rest()
                if n == N:
                    pe.wait_ge(s_max, N - 1)
                    outputT(0)
                if n == N + 1:
                    pe.wait_ge(s_max, N)
                    outputT(1)
                    pe.wait_ge(pt_cp, N - 1)
                    outputT(2)

            def branch(t, n):
                part, half = n // 2, n % 2
                pe.wait_ge(ot_cp, 2 * part + t + 1)
                for k in range(4):
                    last = mm(banks[y_bank(t, n)][:, :], oTv[:, 4 * part + k, tok_rows[t]],
                              (wbn, wbm)[part][:, k, half * 512:(half + 1) * 512], k == 0, k == 3)
                last.then_inc(y_mm, 1)

            def mergedT(t):
                for half in range(2):
                    pe.wait_ge(merged, 2 * t + half + 1)
                    for k in range(4):
                        last = tr(banks[mg_bank(t, half)][:, k * P:(k + 1) * P], gt[:, t, (4 * half + k) * P:(4 * half + k + 1) * P])
                    last.then_inc(mg_mm, 1)

            def w_out(t):
                pe.wait_ge(mg_cp, 2 * t + 2)
                for half in range(2):
                    for k in range(KC):
                        last = mm(banks[wo_bank(t, half)][:, :], xTv[:, k, tok_rows[t]], wo[:, k, half * 512:(half + 1) * 512], k == 0, k == KC - 1)
                    last.then_inc(wo_mm, 1)

            def normedT(t):
                for half in range(2):
                    pe.wait_ge(xt2_ready, 2 * t + half + 1)
                    for k in range(4):
                        last = tr(banks[xt2_bank(t, half)][:, k * P:(k + 1) * P],
                                  gt[:, t, DM + (4 * half + k) * P:DM + (4 * half + k + 1) * P])
                    last.then_inc(xt2_mm, 1)


            def query(t, head, p, first=False):
                if not first:
                    pe.wait_ge(q_cp, p)
                for k in range(KC):
                    rhs = wq[:, k, bass.ds(head * 256, 256)]
                    last = mm(banks[4][:, t * 256:(t + 1) * 256], oTv[:, k, tok_rows[t]], rhs, k == 0, k == KC - 1)
                last.then_inc(q_mm, 1)

            def queryT(t, p, first=False):
                pe.wait_ge(q_cp, p + 1)
                if not first:
                    pe.wait_ge(qt_cp, p)
                for half in range(2):
                    last = tr(banks[5][:, t * 256 + half * P:t * 256 + (half + 1) * P], q_tok[t][:, half * P:(half + 1) * P])
                last.then_inc(qt_mm, 1)

            def key_scores(t, p, first=False):
                pe.wait_ge(qt_cp, p + 1)
                if not first:
                    pe.wait_ge(keys_read, p)
                for half in range(2):
                    last = mm(banks[6][:, t * 256 + half * P:t * 256 + (half + 1) * P], q_T[t][:, half * P:(half + 1) * P],
                              skT[:, half * P:(half + 1) * P])
                last.then_inc(key_mm, 1)

            def weigh(t, k, s, stop=False, nth=None):
                pe.wait_ge(diag_ready, s * SLOTS + (k if nth is None else nth) + 1)
                pe.wait_ge(up_in[k % RING], (2 * s + k // RING + 1) * 16)
                for half in range(2):
                    last = mm(banks[2 * t + half][:, :], diag[:, k % RING, :], ring_up[:, k % RING, half * 512:(half + 1) * 512],
                              False, stop)
                last.then_inc(up_used, 1)

            def half_step(t, s, head, prepare, stop=False):
                if prepare:
                    query(t, head, s + 2)
                for k in range(SLOTS):
                    if k == 4 and prepare:
                        queryT(t, s + 2)
                    if k == 8 and prepare:
                        key_scores(t, s + 2)
                    weigh(t, k, s, stop and k == SLOTS - 1)

            pe.wait_ge(wbn_in, 16)
            pe.wait_ge(wbm_in, 16)
            pe.wait_ge(a_cp, 22)
            branch(0, 0)
            pe.wait_ge(pt_cp, N)
            outputT(3)
            for n in range(1, 4):
                branch(0, n)
            mergedT(0)
            pe.wait_ge(wo_in, 16)
            w_out(0)
            branch(1, 0)
            normedT(0)
            pe.wait_ge(xt2_cp, 2)
            pe.wait_ge(wq_in, 16)
            query(0, 0, 0, first=True)
            queryT(0, 0, first=True)
            key_scores(0, 0, first=True)
            for n in range(1, 4):
                branch(1, n)
            mergedT(1)
            pe.wait_ge(y_used, 8)
            w_out(1)
            pe.wait_ge(y_zero, 1)
            pe.wait_ge(h_ready, 4)
            for b in range(4):
                last = mm(banks[b][:, :], diag[:, 0, :], diag[:, 0:4, :], True, False)
            last.then_inc(y_started, 1)
            pe.wait_ge(keys_read, 1)
            normedT(1)
            pe.wait_ge(xt2_cp, 4)
            query(1, 0, 1)
            weigh(0, 0, 0)
            queryT(1, 1)
            weigh(0, 1, 0)
            key_scores(1, 1)
            for k in range(2, SLOTS):
                if k == 8:
                    query(0, 1, 2)
                if k == 9:
                    queryT(0, 2)
                if k == 10:
                    key_scores(0, 2)
                weigh(0, k, 0)
            half_step(1, 1, 1, True)
            with pe.Fori(1, LOOPS) as i:
                half_step(0, 2 * i, i + 1, True)
                half_step(1, 2 * i + 1, i + 1, True)
            half_step(0, LAST - 1, 0, False, stop=True)
            pe.wait_ge(up_used, LAST * SLOTS)
            pe.sem_inc(y_done, 1)
            for nth, k in enumerate(WEIGHED):
                weigh(1, k, LAST, stop=k == WEIGHED[-1], nth=nth)
            pe.wait_ge(up_used, LAST * SLOTS + len(WEIGHED))
            pe.sem_inc(y_done, 1)


_NAMES = {"w_in": "w_in", "norm1_g": "norm1_g", "pos_k": "nsa_cmp_pos_k", "w1k": "nsa_cmp_w1_k", "w2k": "nsa_cmp_w2_k",
          "pos_v": "nsa_cmp_pos_v", "w1v": "nsa_cmp_w1_v", "w2v": "nsa_cmp_w2_v", "mla_q_norm_g": "mla_q_norm_g",
          "mla_kv_norm_g": "mla_kv_norm_g", "w_uq": "mla_w_uq", "w_ukv": "mla_w_ukv", "wb_nsa": "w_branch_nsa",
          "wb_mla": "w_branch_mla", "w_out": "w_out", "norm2_g": "norm2_g", "w_query": "peer_w_query",
          "sub_keys_1": "peer_sub_keys_1", "sub_keys_2": "peer_sub_keys_2", "expert_down": "peer_expert_down",
          "expert_up": "peer_expert_up", "norm_f_g": "norm_f_g", "x": "x", "positions": "positions"}


def kernel(**inputs):
    import concourse.bacc as bacc
    from concourse.bass_utils import run_bass_kernel_spmd as run

    nc = bacc.Bacc("TRN2", target_bir_lowering=False, num_devices=1)
    arrays, args = {}, {}
    for short, name in _NAMES.items():
        v = np.ascontiguousarray(inputs[name])
        if v.ndim == 3:
            v = v[0]
        arrays[f"in_{short}"] = v
        args[short] = nc.dram_tensor(f"in_{short}", v.shape, mybir.dt.from_np(v.dtype), kind="ExternalInput").ap()
    out = nc.dram_tensor("out", (TOK, DM), F32, kind="ExternalOutput").ap()
    block_program(nc, args, out)
    r = run(nc, [arrays], core_ids=[0])
    return r.results[0]["out"].reshape(1, TOK, DM)
```
